# Optimizing a Trainium2 kernel written in Bass

```python
import jax
import jax.numpy as jnp
from jax import lax
import numpy as np

D_MODEL = 1024
BATCH = 1
SEQ = 2048
DEPTH = 1

GRID_W = 64
CTX_LEN = 256

N_MIXERS = 3
N_ATTN_LAYERS = len(range(0, DEPTH, N_MIXERS))
N_LRU_LAYERS = len(range(1, DEPTH, N_MIXERS))
N_CONV_LAYERS = len(range(2, DEPTH, N_MIXERS))

HEAD_DIM = 64
N_HEADS = D_MODEL // HEAD_DIM
N_KV_HEADS = 4
GROUP = N_HEADS // N_KV_HEADS
WINDOW = 128
BLOCK = 128
ROPE_BASE = 10000.0

D_RNN = D_MODEL
LRU_BLOCK_W = 256
N_LRU_BLOCKS = D_RNN // LRU_BLOCK_W
LRU_CONV_W = 4
LRU_CONV_PAD = (LRU_CONV_W // 2, LRU_CONV_W - 1 - LRU_CONV_W // 2)
LRU_C = 8.0

CONV_K = 31
CONV_PAD = (CONV_K // 2, CONV_K // 2)

N_EXPERTS = 16
D_FF_EXPERT = 2 * D_MODEL
EC_CAPACITY_FACTOR = 2

DEEPNORM_ALPHA = (2 * DEPTH) ** 0.25
DEEPNORM_BETA = (8 * DEPTH) ** -0.25
LN_EPS = 1e-5
NEG_INF = -1e30

kernel_name = "hybrid_interleaved_diffusion_trunk"

def layer_norm(x, g, b):
    xf = x.astype(jnp.float32)
    mu = jnp.mean(xf, axis=-1, keepdims=True)
    var = jnp.mean(jnp.square(xf - mu), axis=-1, keepdims=True)
    y = (xf - mu) * lax.rsqrt(var + LN_EPS) * g.astype(jnp.float32) + b.astype(jnp.float32)
    return y.astype(x.dtype)

def depthwise_conv(x, w, b, pad):
    y = lax.conv_general_dilated(
        x, w[:, None, :], window_strides=(1,), padding=[pad],
        dimension_numbers=("NWC", "WIO", "NWC"), feature_group_count=x.shape[-1])
    return y + b

def axial_rope_tables(n):
    rows = n // GRID_W
    row = jnp.broadcast_to(jnp.arange(rows, dtype=jnp.float32)[:, None], (rows, GRID_W)).reshape(-1)
    col = jnp.broadcast_to(jnp.arange(GRID_W, dtype=jnp.float32)[None, :], (rows, GRID_W)).reshape(-1)
    n_freq = HEAD_DIM // 4
    inv = ROPE_BASE ** (-jnp.arange(n_freq, dtype=jnp.float32) / n_freq)
    ang = jnp.concatenate([row[:, None] * inv, col[:, None] * inv], axis=-1)
    return jnp.cos(ang), jnp.sin(ang)

def apply_rope(t, cos, sin):
    tf = t.astype(jnp.float32)
    t1, t2 = tf[..., :HEAD_DIM // 2], tf[..., HEAD_DIM // 2:]
    cs, sn = cos[None, :, None, :], sin[None, :, None, :]
    return jnp.concatenate([t1 * cs - t2 * sn, t2 * cs + t1 * sn], axis=-1).astype(t.dtype)

def split_qkv(t, w_qkv):
    bsz, n, _ = t.shape
    q_w, kv_w = N_HEADS * HEAD_DIM, N_KV_HEADS * HEAD_DIM
    z = t @ w_qkv
    q = z[..., :q_w].reshape(bsz, n, N_HEADS, HEAD_DIM)
    k = z[..., q_w:q_w + kv_w].reshape(bsz, n, N_KV_HEADS, HEAD_DIM)
    v = z[..., q_w + kv_w:].reshape(bsz, n, N_KV_HEADS, HEAD_DIM)
    return q, k, v

def windowed_sink_gqa(u, uc, w_qkv, sink, w_o, cos, sin, need_ctx):
    bsz, n, _ = u.shape
    scale = HEAD_DIM ** -0.5
    q, k, v = split_qkv(u, w_qkv)
    q = (apply_rope(q, cos, sin) * scale).reshape(bsz, n, N_KV_HEADS, GROUP, HEAD_DIM)
    k = apply_rope(k, cos, sin)
    qc, kc, vc = split_qkv(uc, w_qkv)
    n_ctx = kc.shape[1]
    span = BLOCK + 2 * WINDOW
    kp = jnp.pad(k, ((0, 0), (WINDOW, WINDOW), (0, 0), (0, 0)))
    vp = jnp.pad(v, ((0, 0), (WINDOW, WINDOW), (0, 0), (0, 0)))
    sink_logit = sink.astype(jnp.float32).reshape(1, N_KV_HEADS, GROUP, 1, 1)

    def attend_block(start):
        qb = lax.dynamic_slice_in_dim(q, start, BLOCK, axis=1)
        kb = lax.dynamic_slice_in_dim(kp, start, span, axis=1)
        vb = lax.dynamic_slice_in_dim(vp, start, span, axis=1)
        qpos = start + jnp.arange(BLOCK)
        kpos = start - WINDOW + jnp.arange(span)
        valid = (jnp.abs(qpos[:, None] - kpos[None, :]) <= WINDOW) & (kpos >= 0) & (kpos < n)
        s_loc = jnp.einsum("bqhgd,bkhd->bhgqk", qb, kb).astype(jnp.float32)
        s_loc = jnp.where(valid, s_loc, NEG_INF)
        s_ctx = jnp.einsum("bqhgd,bchd->bhgqc", qb, kc).astype(jnp.float32)
        sinks = jnp.broadcast_to(sink_logit, s_ctx.shape[:-1] + (1,))
        p = jax.nn.softmax(jnp.concatenate([s_ctx, s_loc, sinks], axis=-1), axis=-1).astype(v.dtype)
        return (jnp.einsum("bhgqc,bchd->bqhgd", p[..., :n_ctx], vc)
                + jnp.einsum("bhgqk,bkhd->bqhgd", p[..., n_ctx:n_ctx + span], vb))

    o = lax.map(attend_block, jnp.arange(n // BLOCK) * BLOCK)
    y = jnp.moveaxis(o, 0, 1).reshape(bsz, n, N_HEADS * HEAD_DIM) @ w_o
    yc = None
    if need_ctx:
        qcg = (qc * scale).reshape(bsz, n_ctx, N_KV_HEADS, GROUP, HEAD_DIM)
        s = jnp.einsum("bqhgd,bchd->bhgqc", qcg, kc).astype(jnp.float32)
        sinks = jnp.broadcast_to(sink_logit, s.shape[:-1] + (1,))
        p = jax.nn.softmax(jnp.concatenate([s, sinks], axis=-1), axis=-1)[..., :n_ctx].astype(vc.dtype)
        yc = jnp.einsum("bhgqc,bchd->bqhgd", p, vc).reshape(bsz, n_ctx, N_HEADS * HEAD_DIM) @ w_o
    return y, yc

def rglru_coeffs(xr, gate_a_w, gate_a_b, gate_x_w, gate_x_b, lam, reset_pos):
    bsz, n, _ = xr.shape
    xb = xr.reshape(bsz, n, N_LRU_BLOCKS, LRU_BLOCK_W)
    r = jax.nn.sigmoid((jnp.einsum("bsnc,ncd->bsnd", xb, gate_a_w).reshape(bsz, n, D_RNN)
                        + gate_a_b).astype(jnp.float32))
    i = jax.nn.sigmoid((jnp.einsum("bsnc,ncd->bsnd", xb, gate_x_w).reshape(bsz, n, D_RNN)
                        + gate_x_b).astype(jnp.float32))
    log_a = -LRU_C * r * jax.nn.softplus(-lam.astype(jnp.float32))
    a = jnp.exp(log_a)
    mult = jnp.sqrt(-jnp.expm1(2.0 * log_a))
    if reset_pos is not None:
        mult = jnp.where(jnp.arange(n)[None, :, None] == reset_pos, 1.0, mult)
    return a, mult * i * xr.astype(jnp.float32)

def linear_scan(a, b, h0, reverse):
    if h0 is not None:
        edge = -1 if reverse else 0
        b = b.at[:, edge].add(a[:, edge] * h0)

    def combine(first, second):
        return first[0] * second[0], second[0] * first[1] + second[1]

    _, h = lax.associative_scan(combine, (a, b), reverse=reverse, axis=1)
    return h

def rglru_mixer(u, uc, w_in, conv_w, conv_b, gate_a_w, gate_a_b, gate_x_w, gate_x_b, lam, w_out,
                need_ctx):
    n_ctx = uc.shape[1]

    def branches(t):
        gate, rec = jnp.split(t @ w_in, 2, axis=-1)
        return jax.nn.gelu(gate), depthwise_conv(rec, conv_w, conv_b, LRU_CONV_PAD)

    g, xr = branches(u)
    gc, xrc = branches(uc)
    a_cf, b_cf = rglru_coeffs(xrc, gate_a_w[0], gate_a_b[0], gate_x_w[0], gate_x_b[0], lam[0], 0)
    a_cb, b_cb = rglru_coeffs(xrc, gate_a_w[1], gate_a_b[1], gate_x_w[1], gate_x_b[1], lam[1], n_ctx - 1)
    hc_f = linear_scan(a_cf, b_cf, None, False)
    hc_b = linear_scan(a_cb, b_cb, None, True)
    a_f, b_f = rglru_coeffs(xr, gate_a_w[0], gate_a_b[0], gate_x_w[0], gate_x_b[0], lam[0], None)
    a_b, b_b = rglru_coeffs(xr, gate_a_w[1], gate_a_b[1], gate_x_w[1], gate_x_b[1], lam[1], None)
    h_f = linear_scan(a_f, b_f, hc_f[:, -1], False)
    h_b = linear_scan(a_b, b_b, hc_b[:, 0], True)
    y = ((h_f + h_b).astype(u.dtype) * g) @ w_out
    yc = (((hc_f + hc_b).astype(uc.dtype) * gc) @ w_out) if need_ctx else None
    return y, yc

def conformer_conv(u, uc, w_in, b_in, dw_w, dw_b, ln_g, ln_b, w_out, b_out, need_ctx):
    def module(t):
        val, gt = jnp.split(t @ w_in + b_in, 2, axis=-1)
        z = val * jax.nn.sigmoid(gt)
        z = depthwise_conv(z, dw_w, dw_b, CONV_PAD)
        z = jax.nn.silu(layer_norm(z, ln_g, ln_b))
        return z @ w_out + b_out

    return module(u), (module(uc) if need_ctx else None)

def expert_choice_ffn(t, router, w1, w3, w2):
    bsz, n, dm = t.shape
    cap = max(1, EC_CAPACITY_FACTOR * n // N_EXPERTS)
    aff = jax.nn.softmax((t @ router).astype(jnp.float32), axis=-1)
    gate, idx = lax.top_k(jnp.swapaxes(aff, 1, 2), cap)
    xg = jax.vmap(lambda tb, ib: tb[ib])(t, idx)
    hid = jax.nn.silu(jnp.einsum("becd,edf->becf", xg, w1)) * jnp.einsum("becd,edf->becf", xg, w3)
    y = jnp.einsum("becf,efd->becd", hid, w2) * gate[..., None].astype(t.dtype)
    return jax.vmap(lambda yb, ib: jnp.zeros((n, dm), yb.dtype).at[ib.reshape(-1)].add(
        yb.reshape(-1, dm)))(y, idx)

def setup_inputs(seed: int = 0) -> dict:
    key = jax.random.key(seed)
    ks = iter(jax.random.split(key, 40))
    f32 = jnp.float32
    D, E, F = D_MODEL, N_EXPERTS, D_FF_EXPERT

    def nrm(shape, scale):
        return jax.random.normal(next(ks), shape, f32) * scale

    def gain(shape):
        return 1.0 + nrm(shape, 0.02)

    qkv_w = (N_HEADS + 2 * N_KV_HEADS) * HEAD_DIM
    a_c = jax.random.uniform(next(ks), (N_LRU_LAYERS, 2, D_RNN), f32, 0.9, 0.999)
    a_base = a_c ** (1.0 / LRU_C)
    lru_lambda = jnp.log(a_base) - jnp.log1p(-a_base)
    return {
        "x": nrm((BATCH, SEQ, D), 1.0),
        "c": nrm((BATCH, D), 1.0),
        "ctx": nrm((BATCH, CTX_LEN, D), 1.0),
        "c_ctx": nrm((D,), 1.0),
        "ada_w": nrm((DEPTH, D, 6 * D), 0.5 * D ** -0.5),
        "ada_b": nrm((DEPTH, 6 * D), 0.02),
        "ln1_g": gain((DEPTH, D)),
        "ln1_b": nrm((DEPTH, D), 0.02),
        "ln2_g": gain((DEPTH, D)),
        "ln2_b": nrm((DEPTH, D), 0.02),
        "attn_w_qkv": nrm((N_ATTN_LAYERS, D, qkv_w), D ** -0.5),
        "attn_sink": nrm((N_ATTN_LAYERS, N_HEADS), 1.0),
        "attn_w_o": nrm((N_ATTN_LAYERS, N_HEADS * HEAD_DIM, D), DEEPNORM_BETA * D ** -0.5),
        "lru_w_in": nrm((N_LRU_LAYERS, D, 2 * D_RNN), D ** -0.5),
        "lru_conv_w": nrm((N_LRU_LAYERS, LRU_CONV_W, D_RNN), LRU_CONV_W ** -0.5),
        "lru_conv_b": nrm((N_LRU_LAYERS, D_RNN), 0.02),
        "lru_gate_a_w": nrm((N_LRU_LAYERS, 2, N_LRU_BLOCKS, LRU_BLOCK_W, LRU_BLOCK_W), LRU_BLOCK_W ** -0.5),
        "lru_gate_a_b": nrm((N_LRU_LAYERS, 2, D_RNN), 0.02),
        "lru_gate_x_w": nrm((N_LRU_LAYERS, 2, N_LRU_BLOCKS, LRU_BLOCK_W, LRU_BLOCK_W), LRU_BLOCK_W ** -0.5),
        "lru_gate_x_b": nrm((N_LRU_LAYERS, 2, D_RNN), 0.02),
        "lru_lambda": lru_lambda,
        "lru_w_out": nrm((N_LRU_LAYERS, D_RNN, D), DEEPNORM_BETA * D_RNN ** -0.5),
        "conv_w_in": nrm((N_CONV_LAYERS, D, 2 * D), D ** -0.5),
        "conv_b_in": nrm((N_CONV_LAYERS, 2 * D), 0.02),
        "conv_dw_w": nrm((N_CONV_LAYERS, CONV_K, D), CONV_K ** -0.5),
        "conv_dw_b": nrm((N_CONV_LAYERS, D), 0.02),
        "conv_ln_g": gain((N_CONV_LAYERS, D)),
        "conv_ln_b": nrm((N_CONV_LAYERS, D), 0.02),
        "conv_w_out": nrm((N_CONV_LAYERS, D, D), DEEPNORM_BETA * D ** -0.5),
        "conv_b_out": nrm((N_CONV_LAYERS, D), 0.02),
        "moe_router": nrm((DEPTH, D, E), D ** -0.5),
        "moe_w1": nrm((DEPTH, E, D, F), D ** -0.5),
        "moe_w3": nrm((DEPTH, E, D, F), D ** -0.5),
        "moe_w2": nrm((DEPTH, E, F, D), DEEPNORM_BETA * F ** -0.5),
    }

def reference(x, c, ctx, c_ctx, ada_w, ada_b, ln1_g, ln1_b, ln2_g, ln2_b,
              attn_w_qkv, attn_sink, attn_w_o,
              lru_w_in, lru_conv_w, lru_conv_b, lru_gate_a_w, lru_gate_a_b, lru_gate_x_w,
              lru_gate_x_b, lru_lambda, lru_w_out,
              conv_w_in, conv_b_in, conv_dw_w, conv_dw_b, conv_ln_g, conv_ln_b, conv_w_out, conv_b_out,
              moe_router, moe_w1, moe_w3, moe_w2):
    cos, sin = axial_rope_tables(x.shape[1])
    h = ctx
    silu_c = jax.nn.silu(c)
    silu_cc = jax.nn.silu(c_ctx)
    for i in range(DEPTH):
        need_ctx = i < DEPTH - 1
        kind, j = i % N_MIXERS, i // N_MIXERS
        mod = silu_c @ ada_w[i] + ada_b[i]
        mod_c = silu_cc @ ada_w[i] + ada_b[i]
        sh1, sc1, g1, sh2, sc2, g2 = jnp.split(mod[:, None, :], 6, axis=-1)
        csh1, csc1, cg1, csh2, csc2, cg2 = jnp.split(mod_c, 6)
        u = x * (1 + sc1) + sh1
        uc = h * (1 + csc1) + csh1
        if kind == 0:
            y, yc = windowed_sink_gqa(u, uc, attn_w_qkv[j], attn_sink[j], attn_w_o[j], cos, sin, need_ctx)
        elif kind == 1:
            y, yc = rglru_mixer(u, uc, lru_w_in[j], lru_conv_w[j], lru_conv_b[j], lru_gate_a_w[j],
                                lru_gate_a_b[j], lru_gate_x_w[j], lru_gate_x_b[j], lru_lambda[j],
                                lru_w_out[j], need_ctx)
        else:
            y, yc = conformer_conv(u, uc, conv_w_in[j], conv_b_in[j], conv_dw_w[j], conv_dw_b[j],
                                   conv_ln_g[j], conv_ln_b[j], conv_w_out[j], conv_b_out[j], need_ctx)
        x = layer_norm(DEEPNORM_ALPHA * x + g1 * y, ln1_g[i], ln1_b[i])
        f = expert_choice_ffn(x * (1 + sc2) + sh2, moe_router[i], moe_w1[i], moe_w3[i], moe_w2[i])
        x = layer_norm(DEEPNORM_ALPHA * x + g2 * f, ln2_g[i], ln2_b[i])
        if need_ctx:
            h = layer_norm(DEEPNORM_ALPHA * h + cg1 * yc, ln1_g[i], ln1_b[i])
            fc = expert_choice_ffn(h * (1 + csc2) + csh2, moe_router[i], moe_w1[i], moe_w3[i], moe_w2[i])
            h = layer_norm(DEEPNORM_ALPHA * h + cg2 * fc, ln2_g[i], ln2_b[i])
    return x


_drawn_inputs = setup_inputs


def setup_inputs(seed=0):
    import zlib

    import numpy as np

    out = dict(_drawn_inputs(seed))
    spreads = {}
    factors = {'ctx': 5.241,
     'ada_b': 8.0,
     'ln1_g': 2.84,
     'ln1_b': 2.979,
     'ln2_g': 8.343,
     'ln2_b': 8.341,
     'attn_sink': 28.13}
    for name, (base, spread) in spreads.items():
        noise = np.random.default_rng([zlib.crc32(name.encode()), seed]).standard_normal(out[name].shape)
        drawn = base * np.exp(spread * noise) if base else spread * noise
        out[name] = jnp.asarray(drawn.astype(out[name].dtype))
    for name, factor in factors.items():
        out[name] = (out[name] * factor).astype(out[name].dtype)
    return out
```

```python
from contextlib import ExitStack

import concourse.bass as bass
from concourse import mybir

F32 = mybir.dt.float32
F32R = mybir.dt.float32r
BF16 = mybir.dt.bfloat16
F16 = mybir.dt.float16
U32 = mybir.dt.uint32
I32 = mybir.dt.int32
ALU = mybir.AluOpType
ACT = mybir.ActivationFunctionType
AX_X = mybir.AxisListType.X

P = 128
BANK = 512
NEG = -1e30


class Dims:

    def __init__(self, x, ctx, ada_w, attn_w_qkv, attn_sink, moe_router, moe_w1):
        _, self.T, self.D = x.shape
        self.CTX = ctx.shape[1]
        self.H = attn_sink.shape[1]
        self.DH = self.D // self.H
        self.QKV = attn_w_qkv.shape[2]
        self.G = (self.QKV // self.DH - self.H) // 2
        self.HG = self.H // self.G
        self.E = moe_router.shape[2]
        self.F = moe_w1.shape[3]
        self.CAP = 2 * self.T // self.E
        self.NT = self.T // P
        self.NC = self.CTX // P
        self.KD = self.D // P
        self.MOD = ada_w.shape[2]
        self.WIN = 3 * P
        self.alpha = 2.0 ** 0.25
        self.eps = 1e-5
        assert self.DH == 64 and self.G == 4 and self.HG == 4 and self.QKV == 3 * BANK
        assert self.D == 2 * BANK and self.CTX == 2 * P and self.CAP == 2 * P and self.F == 4 * BANK


def wait(eng, sem, value):
    if isinstance(value, int) and value <= 0:
        return
    eng.wait_ge(sem, value)


def apart(eng, carried):
    eng.sem_inc(carried, 1)


def peeled(eng, n, body):
    body(0)
    with eng.Fori(1, n) as i:
        body(i)


def copies(ap, dim, n):
    shape = list(ap.shape)
    return ap.unsqueeze(dim).broadcast_to(shape[:dim] + [n] + shape[dim:])



def modulation(nc, d, io, scratch, const, wqkv_hi, wqkv_lo):
    RING = 3
    NCH = d.MOD // BANK
    ada = io["ada_w"][0].rearrange("(p k) n -> p k n", k=d.KD)
    wq = io["attn_w_qkv"][0].rearrange("(k p) n -> p k n", p=P)
    with ExitStack() as ctx:
        sb = lambda n, s, t=F32: ctx.enter_context(nc.sbuf_tensor(n, s, t))
        sem = lambda n: ctx.enter_context(nc.semaphore(n))
        c_in = sb("c_in", [P, 2, d.KD])
        c_act = sb("c_act", [P, 2, d.KD])
        ada_raw = [sb(f"ada_raw{q}", [P, d.KD, BANK]) for q in range(RING)]
        bias = [sb(f"bias{q}", [2, BANK]) for q in range(RING)]
        mod = [sb(f"mod{q}", [2, BANK]) for q in range(RING)]
        w_raw = sb("w_raw", [P, d.KD, BANK])
        ps = [ctx.enter_context(nc.psum_tensor(f"mod_ps{q}", [P, BANK], F32)) for q in range(RING)]
        c_loaded, c_ready = sem("c_loaded"), sem("c_ready")
        ada_loaded = [sem(f"ada_loaded{q}") for q in range(RING)]
        mod_summed, mod_ready = sem("mod_summed"), sem("mod_ready")
        mod_stored = [sem(f"mod_stored{q}") for q in range(RING)]
        w_loaded, w_hi_done, w_lo_done = sem("w_loaded"), sem("w_hi_done"), sem("w_lo_done")
        block = ctx.enter_context(nc.Block())

        @block.sync
        def _(sp):
            sp.dma_start(c_in[:, 0, :], io["c"][0].rearrange("(p k) -> p k", k=d.KD)).then_inc(c_loaded, 16)
            sp.dma_start(c_in[:, 1, :], io["c_ctx"].rearrange("(p k) -> p k", k=d.KD)).then_inc(c_loaded, 16)

            def chunks(j):
                for q in range(RING):
                    n = RING * j + q
                    wait(sp, mod_summed, RING * (j - 1) + q + 1)
                    sp.dma_start(ada_raw[q][:], ada[:, :, bass.ds(n * BANK, BANK)]).then_inc(ada_loaded[q], 16)
                    wait(sp, mod_ready, RING * (j - 1) + q + 1)
                    sp.dma_start(bias[q][:], io["ada_b"][0:1, bass.ds(n * BANK, BANK)]
                                 .broadcast_to([2, BANK])).then_inc(ada_loaded[q], 16)
            peeled(sp, NCH // RING, chunks)

        @block.gpsimd
        def _(pool):
            def store(j):
                for q in range(RING):
                    pool.wait_ge(mod_ready, RING * j + q + 1)
                    pool.dma_start(scratch["mod"][:, bass.ds((RING * j + q) * BANK, BANK)],
                                   mod[q][:]).then_inc(mod_stored[q], 16)
            peeled(pool, NCH // RING, store)
            for q in range(RING):
                pool.wait_ge(mod_stored[q], 16 * (NCH // RING))

        @block.scalar
        def _(act):
            act.wait_ge(c_loaded, 32)
            act.activation(c_act[:], c_in[:], ACT.Silu).then_inc(c_ready, 1)
            for n in range(d.QKV // BANK):
                wait(act, w_hi_done, n)
                wait(act, w_lo_done, n)
                act.dma_start(w_raw[:], wq[:, :, n * BANK:(n + 1) * BANK]).then_inc(w_loaded, 16)
                act.wait_ge(w_loaded, 16 * (n + 1))
                act.activation(wqkv_hi[:, :, n * BANK:(n + 1) * BANK], w_raw[:], ACT.Copy).then_inc(w_hi_done, 1)

        @block.tensor
        def _(pe):
            pe.wait_ge(c_ready, 1)

            def chunks(j):
                for q in range(RING):
                    pe.wait_ge(ada_loaded[q], 32 * (j + 1))
                    wait(pe, mod_ready, RING * (j - 1) + q + 1)
                    for k in range(d.KD):
                        last = pe.matmul(ps[q][0:2, :], c_act[:, :, k], ada_raw[q][:, k, :],
                                         start=(k == 0), stop=(k == d.KD - 1))
                    last.then_inc(mod_summed, 1)
            peeled(pe, NCH // RING, chunks)

        @block.vector
        def _(dve):
            def chunks(j):
                for q in range(RING):
                    dve.wait_ge(mod_summed, RING * j + q + 1)
                    wait(dve, mod_stored[q], 16 * j)
                    dve.tensor_tensor(mod[q][:], ps[q][0:2, :], bias[q][:], ALU.add).then_inc(mod_ready, 1)
                if isinstance(j, int):
                    for n in range(d.QKV // BANK):
                        dve.wait_ge(w_hi_done, n + 1)
                        cols = slice(n * BANK, (n + 1) * BANK)
                        dve.tensor_tensor(wqkv_lo[:, :, cols], w_raw[:], wqkv_hi[:, :, cols].bitcast(F32),
                                          ALU.subtract).then_inc(w_lo_done, 1)
            peeled(dve, NCH // RING, chunks)



def projection(nc, d, io, scratch, const, wqkv_hi, wqkv_lo, k_ctx, v_ctx):
    S0, S1 = d.NC, d.NC + d.NT
    HK = d.H + d.G
    ROT = HK * d.DH
    HALF = d.DH // 2
    FILL = 4
    NB = 3

    def fills_before(s):
        return 2 * s if isinstance(s, int) and s <= S0 else 2 * S0 + 6 * (s - S0)

    with ExitStack() as ctx:
        sb = lambda n, s, t=F32: ctx.enter_context(nc.sbuf_tensor(n, s, t))
        psum = lambda n, s: ctx.enter_context(nc.psum_tensor(n, s, F32))
        sem = lambda n: ctx.enter_context(nc.semaphore(n))
        rows = sb("mod_rows", [P, 4, d.D])
        x_in = [sb(f"x_in{b}", [P, d.D]) for b in range(2)]
        x_mod = [sb(f"x_mod{b}", [P, d.D]) for b in range(2)]
        u_hi = [sb(f"u_hi{b}", [P, d.KD, P], F32R) for b in range(2)]
        u_lo = [sb(f"u_lo{b}", [P, d.KD, P], F32R) for b in range(2)]
        cos = sb("cos", [P, d.NT, d.DH])
        sin = sb("sin", [P, d.NT, d.DH])
        rot_a = sb("rot_a", [P, HK, d.DH])
        rot_b = sb("rot_b", [P, HK, d.DH])
        q_split = sb("q_split", [P, d.H, 2, d.DH], F32R)
        k_split = sb("k_split", [P, d.G, 2, 2, d.DH], F32R)
        v_split = sb("v_split", [P, d.G, 2, d.DH], F32R)
        qt_out = sb("qt_out", [P, d.H, P])
        kt_out = sb("kt_out", [P, d.G, 2, P])
        ps_x = psum("ps_x", [P, d.KD, P])
        ps_q = psum("ps_q", [P, d.QKV])
        ps_t = [psum(f"ps_t{b}", [P, FILL, P]) for b in range(NB)]
        rows_loaded, rows_ready, tables_loaded = sem("rows_loaded"), sem("rows_ready"), sem("tables_loaded")
        x_loaded = [sem(f"x_loaded{b}") for b in range(2)]
        scaled, modulated = sem("scaled"), sem("modulated")
        x_turned, u_hi_done, u_lo_done = sem("x_turned"), sem("u_hi_done"), sem("u_lo_done")
        projected, rotated, v_hi_done, added = sem("projected"), sem("rotated"), sem("v_hi_done"), sem("added")
        hi_done, lo_done = sem("hi_done"), sem("lo_done")
        turned, moved = sem("turned"), sem("moved")
        q_stored, k_stored, v_stored = sem("q_stored"), sem("k_stored"), sem("v_stored")
        zeroed, pads_stored = sem("zeroed"), sem("pads_stored")
        block = ctx.enter_context(nc.Block())

        def run(eng, step, ahead=0):
            for s in range(S0 + 2):
                step(s, s % 2)
            with eng.Fori(0, (d.NT - 2) // 2 - ahead) as j:
                for b in range(2):
                    step(S0 + 2 + 2 * j + b, b)
            for s in range(S1 - 2 * ahead, S1 + 2):
                step(s, s % 2)

        def is_latent(s):
            return not isinstance(s, int) or s >= S0

        def in_range(s):
            return not isinstance(s, int) or 0 <= s < S1

        def fill_plan(s):
            ks = [(False, 0), (False, 2)]
            return ks + [(True, h) for h in range(0, d.H, FILL)] if is_latent(s) else ks

        def bank_of(s, f):
            before = fills_before(s) if isinstance(s, int) else fills_before(S0)
            return (before + f) % NB

        @block.sync
        def _(sp):
            for r, (stream, part) in enumerate([(0, 1), (0, 0), (1, 1), (1, 0)]):
                sp.dma_start(rows[:, r, :], scratch["mod"][stream:stream + 1, part * d.D:(part + 1) * d.D]
                             .broadcast_to([P, d.D])).then_inc(rows_loaded, 16)
            sp.dma_start(cos[:], io["cos"].rearrange("(t p) h -> p t h", p=P)).then_inc(tables_loaded, 16)
            sp.dma_start(sin[:], io["sin"].rearrange("(t p) h -> p t h", p=P)).then_inc(tables_loaded, 16)
            sp.wait_ge(zeroed, 1)
            for t in (0, d.NT + 1):
                sp.dma_start(scratch["kt"][:, :, :, t * P:(t + 1) * P],
                             qt_out[:, 0:2 * d.G, :].rearrange("p (g s) n -> p g s n", s=2)).then_inc(pads_stored, 16)
                sp.dma_start(scratch["v"][t], qt_out[:, 0:d.G, :]).then_inc(pads_stored, 16)

            def load(s, b):
                wait(sp, modulated, s - 1)
                src = io["x"][0, bass.ds((s - S0) * P, P), :] if is_latent(s) else io["ctx"][0, s * P:(s + 1) * P, :]
                sp.dma_start(x_in[b][:], src).then_inc(x_loaded[b], 16)

            load(0, 0)

            def step(s, b):
                if in_range(s + 1):
                    load(s + 1, 1 - b)
                t = s - 2
                if in_range(t) and is_latent(t):
                    lt = t - S0
                    sp.wait_ge(hi_done, t + 1)
                    sp.wait_ge(lo_done, t + 1)
                    sp.dma_start(scratch["v"][bass.ds(lt + 1, 1)].rearrange("t p g n -> (t p) g n"),
                                 v_split[:].rearrange("p g s n -> p g (s n)").bitcast(F32)).then_inc(v_stored, 16)
                    sp.wait_ge(moved, fills_before(t) + 2)
                    sp.dma_start(scratch["kt"][:, :, :, bass.ds((lt + 1) * P, P)], kt_out[:]).then_inc(k_stored, 16)
                    sp.wait_ge(moved, fills_before(t) + 6)
                    sp.dma_start(scratch["qt"][bass.ds(lt, 1)].rearrange("t p h n -> (t p) h n"),
                                 qt_out[:]).then_inc(q_stored, 16)
            run(sp, step, ahead=1)
            sp.wait_ge(pads_stored, 64)
            for s in (q_stored, k_stored, v_stored):
                sp.wait_ge(s, 16 * d.NT)

        @block.gpsimd
        def _(pool):
            pool.wait_ge(rows_ready, 1)

            def modulate(s, b):
                r = 0 if is_latent(s) else 2
                pool.wait_ge(x_loaded[b], 16 * ((s - b) // 2 + 1) if isinstance(s, int) else
                             16 * (S0 // 2 + 1) + 8 * (s - S0 - b))
                wait(pool, x_turned, s - 1)
                pool.tensor_tensor(x_mod[b][:], x_in[b][:], rows[:, r, :], ALU.mult).then_inc(scaled, 1)
                pool.wait_ge(scaled, s + 1)
                pool.tensor_tensor(x_mod[b][:], x_mod[b][:], rows[:, r + 1, :], ALU.add).then_inc(modulated, 1)

            modulate(0, 0)

            def step(s, b):
                if in_range(s + 1):
                    modulate(s + 1, 1 - b)
                t = s - 1
                if in_range(t):
                    pool.wait_ge(rotated, t + 1)
                    k_heads = slice(0, HK) if is_latent(t) else slice(d.H, HK)
                    if is_latent(t):
                        pool.tensor_tensor(rot_a[:, k_heads, :], rot_a[:, k_heads, :], rot_b[:, k_heads, :],
                                           ALU.add).then_inc(added, 1)
                    else:
                        pool.sem_inc(added, 1)
            run(pool, step, ahead=1)

        @block.scalar
        def _(act):
            def step(s, b):
                if in_range(s):
                    act.wait_ge(x_turned, s + 1)
                    wait(act, projected, s - 1)
                    act.activation(u_hi[b][:], ps_x[:], ACT.Copy).then_inc(u_hi_done, 1)
                t = s - 1
                if in_range(t):
                    act.wait_ge(projected, t + 1)
                    act.wait_ge(rotated, t + 1)
                    if is_latent(t):
                        wait(act, v_stored, 16 * (t - S0))
                        v_hi = v_split[:, :, 0, :]
                    else:
                        v_hi = v_ctx[:, t, :, 0:d.DH]
                    act.activation(v_hi, ps_q[:, ROT:d.QKV].rearrange("p (g n) -> p g n", g=d.G),
                                   ACT.Copy).then_inc(v_hi_done, 1)
                t = s - 2
                if in_range(t):
                    if is_latent(t):
                        wait(act, k_stored, 16 * (t - S0))
                        wait(act, q_stored, 16 * (t - S0))
                        act.wait_ge(pads_stored, 64)
                    for f, (is_q, h) in enumerate(fill_plan(t)):
                        bank = ps_t[bank_of(t, f)]
                        act.wait_ge(turned, fills_before(t) + f + 1)
                        if is_q:
                            dst, src = qt_out[:, h:h + FILL, :], bank[:]
                        else:
                            src = bank[:].rearrange("p (g s) n -> p g s n", s=2)
                            dst = kt_out[:, h:h + 2] if is_latent(t) else k_ctx[:, h:h + 2, :, t * P:(t + 1) * P]
                        act.activation(dst, src, ACT.Copy, scale=d.DH ** -0.5 if is_q else 1.0).then_inc(moved, 1)
                t = s - 1
                if in_range(t):
                    act.wait_ge(added, t + 1)
                    wait(act, turned, fills_before(t))
                    if is_latent(t):
                        act.activation(q_split[:, :, 0, :], rot_a[:, 0:d.H, :], ACT.Copy)
                    act.activation(k_split[:, :, 0, :, :], copies(rot_a[:, d.H:HK, :], 2, 2),
                                   ACT.Copy).then_inc(hi_done, 1)
            run(act, step)

        @block.vector
        def _(dve):
            dve.memset(qt_out[:, 0:2 * d.G, :], 0.0).then_inc(zeroed, 1)
            dve.wait_ge(rows_loaded, 64)
            dve.tensor_scalar(rows[:, 0:4:2, :], rows[:, 0:4:2, :], 1.0, None, ALU.add).then_inc(rows_ready, 1)
            dve.wait_ge(tables_loaded, 32)

            def step(s, b):
                if in_range(s):
                    dve.wait_ge(u_hi_done, s + 1)
                    wait(dve, projected, s - 1)
                    dve.tensor_tensor(u_lo[b][:], ps_x[:], u_hi[b][:].bitcast(F32), ALU.subtract).then_inc(u_lo_done, 1)
                t = s - 1
                if in_range(t):
                    dve.wait_ge(projected, t + 1)
                    wait(dve, hi_done, t)
                    wait(dve, lo_done, t)
                    heads = ps_q[:, 0:ROT].rearrange("p (h n) -> p h n", n=d.DH)
                    if is_latent(t):
                        wait(dve, added, t)
                        cs = cos[:, bass.ds(t - S0, 1), :].broadcast_to([P, HK, d.DH])
                        dve.tensor_tensor(rot_a[:], heads, cs, ALU.mult)
                        for to, of in ((0, 1), (1, 0)):
                            sn = sin[:, bass.ds(t - S0, 1), to * HALF:(to + 1) * HALF].broadcast_to([P, HK, HALF])
                            last = dve.tensor_tensor(rot_b[:, :, to * HALF:(to + 1) * HALF],
                                                     heads[:, :, of * HALF:(of + 1) * HALF], sn, ALU.mult)
                        last.then_inc(rotated, 1)
                    else:
                        dve.tensor_copy(rot_a[:, d.H:HK, :], heads[:, d.H:HK, :]).then_inc(rotated, 1)
                    dve.wait_ge(v_hi_done, t + 1)
                    if is_latent(t):
                        v_hi, v_lo = v_split[:, :, 0, :], v_split[:, :, 1, :]
                        wait(dve, v_stored, 16 * (t - S0))
                    else:
                        v_hi, v_lo = v_ctx[:, t, :, 0:d.DH], v_ctx[:, t, :, d.DH:2 * d.DH]
                    dve.tensor_tensor(v_lo, ps_q[:, ROT:d.QKV].rearrange("p (g n) -> p g n", g=d.G),
                                      v_hi.bitcast(F32), ALU.subtract)
                    dve.wait_ge(hi_done, t + 1)
                    wait(dve, turned, fills_before(t))
                    if is_latent(t):
                        dve.tensor_tensor(q_split[:, :, 1, :], rot_a[:, 0:d.H, :],
                                          q_split[:, :, 0, :].bitcast(F32), ALU.subtract)
                    dve.tensor_tensor(k_split[:, :, 1, :, :], copies(rot_a[:, d.H:HK, :], 2, 2),
                                      k_split[:, :, 0, :, :].bitcast(F32), ALU.subtract).then_inc(lo_done, 1)
            run(dve, step)

        @block.tensor
        def _(pe):
            def step(s, b):
                if in_range(s):
                    pe.wait_ge(modulated, s + 1)
                    wait(pe, u_lo_done, s)
                    for k in range(d.KD):
                        last = pe.transpose(ps_x[:, k, :], x_mod[b][:, k * P:(k + 1) * P], const["ident"][:])
                    last.then_inc(x_turned, 1)
                t = s - 1
                if in_range(t):
                    c = 1 - b
                    pe.wait_ge(u_lo_done, t + 1)
                    wait(pe, rotated, t)
                    wait(pe, lo_done, t)
                    wait(pe, v_hi_done, t)
                    for n in range(0 if is_latent(t) else 2, 3):
                        cols = slice(n * BANK, (n + 1) * BANK)
                        for k in range(d.KD):
                            for i, (u, w) in enumerate(((u_hi, wqkv_hi), (u_hi, wqkv_lo), (u_lo, wqkv_hi))):
                                last = pe.matmul(ps_q[:, cols], u[c][:, k, :], w[:, k, cols],
                                                 start=(k == 0 and i == 0), stop=(k == d.KD - 1 and i == 2))
                    last.then_inc(projected, 1)
                t = s - 2
                if in_range(t):
                    pe.wait_ge(hi_done, t + 1)
                    pe.wait_ge(lo_done, t + 1)
                    for f, (is_q, h) in enumerate(fill_plan(t)):
                        bank = ps_t[bank_of(t, f)]
                        wait(pe, moved, fills_before(t) + f + 1 - NB)
                        for i in range(FILL):
                            src = q_split[:, h + i, :, :] if is_q else k_split[:, h + i // 2, i % 2, :, :]
                            last = pe.transpose(bank[:, i, :], src.rearrange("p a n -> p (a n)").bitcast(F32),
                                                const["ident"][:])
                        last.then_inc(turned, 1)
            run(pe, step)



def attention(nc, d, io, scratch, const, k_ctx, v_ctx, aff):
    SLOT = 2 * BANK
    W0, W1, C1 = BANK - d.WIN, BANK, BANK + d.CTX
    KEYS = d.WIN + d.CTX
    KB = KEYS // P
    HG, G, NT = d.HG, d.G, d.NT
    LG = BANK // 2
    HP = d.H // 2

    with ExitStack() as ctx:
        sb = lambda n, s, t=F32: ctx.enter_context(nc.sbuf_tensor(n, s, t))
        psum = lambda n, s: ctx.enter_context(nc.psum_tensor(n, s, F32))
        sem = lambda n: ctx.enter_context(nc.semaphore(n))
        wo_raw = sb("wo_raw", [P, HP, BANK // 2])
        wo_hi = sb("wo_hi", [P, HP, d.D], F32R)
        wo_lo = sb("wo_lo", [P, HP, d.D], F32R)
        q_in = [sb(f"q_in{b}", [P, HG, P], F32R) for b in range(2)]
        k_in = [sb(f"k_in{b}", [P, 2, d.WIN], F32R) for b in range(2)]
        v_in = [sb(f"v_in{b}", [P, 3, 2 * d.DH], F32R) for b in range(2)]
        x_in = sb("xa_in", [P, d.D])
        prob = [sb(f"prob{g}", [P, HG, KEYS + 1]) for g in range(G)]
        pt_hi = [sb(f"pt_hi{b}", [P, HG, P], F32R) for b in range(2)]
        pt_lo = [sb(f"pt_lo{b}", [P, HG, P], F32R) for b in range(2)]
        o_low = sb("o_low", [d.DH, HG, P])
        o_sum = sb("o_sum", [P, HP, P])
        o_hi = sb("o_hi", [P, HP, P], F32R)
        o_lo = sb("o_lo", [P, HP, P], F32R)
        z = sb("z", [P, d.D])
        t_out = sb("t_out", [P, d.D])
        r_out = sb("r_out", [P, d.D])
        tt = sb("tt", [P, d.KD, P])
        row_g1 = sb("row_g1", [P, d.D])
        row_tg = sb("row_tg", [P, d.D])
        row_tb = sb("row_tb", [P, d.D])
        row_rg = sb("row_rg", [P, d.D])
        row_rb = sb("row_rb", [P, d.D])
        router = sb("router", [P, d.KD, d.E])
        mask = sb("mask", [P, 3, P], BF16)
        sink = sb("sink", [P, d.H])
        sink_part = [sb(f"sink_part{n}", [P, d.H], BF16) for n in range(3)]
        sink_key = sb("sink_key", [P, d.H], BF16)
        ones = sb("ones3", [P, P], BF16)
        neg_max = [sb(f"neg_max{b}", [P, HG]) for b in range(2)]
        total = [sb(f"total{g}", [P, HG]) for g in range(G)]
        inv = [sb(f"inv{g}", [P, HG]) for g in range(G)]
        stats = sb("stats", [P, 2, 6])
        mean_var = sb("mean_var", [P, 2])
        var_eps = sb("var_eps", [P, 1])
        minus_half = sb("minus_half", [P, 1])
        rstd = sb("rstd", [P, 1])
        lg_t = sb("lg_t", [d.E, P])
        lg_max = sb("lg_max", [P, 1])
        lg_exp = sb("lg_exp", [P, d.E])
        lg_sum = sb("lg_sum", [P, 1])
        lg_inv = sb("lg_inv", [P, 1])
        ps_s = [psum(f"ps_s{b}", [P, SLOT]) for b in range(2)]
        ps_t = [psum(f"ps_pt{b}", [P, HG, P]) for b in range(2)]
        ps_o = psum("ps_o", [P, HG, P])
        ps_y = psum("ps_y", [P, BANK])

        rows_loaded, rows_mid, rows_ready = sem("rows_loaded"), sem("rows_mid"), sem("rows_ready")
        masks_made, sink_ready, half_made = sem("masks_made"), sem("sink_ready"), sem("half_made")
        router_loaded = sem("router_loaded")
        wo_loaded, wo_hi_done, wo_lo_done = sem("wo_loaded"), sem("wo_hi_done"), sem("wo_lo_done")
        qk_loaded = [sem(f"qk_loaded{b}") for b in range(2)]
        v_loaded = [sem(f"v_loaded{b}") for b in range(2)]
        x_loaded = sem("xa_loaded")
        scored, maxed, expd = sem("scored"), sem("maxed"), sem("expd")
        inverted, normed = sem("inverted"), sem("normed")
        turned, pt_hi_done, pt_lo_done, pv_done = sem("p_turned"), sem("pt_hi_done"), sem("pt_lo_done"), sem("pv_done")
        o_copied, o_added, o_hi_done, o_lo_done = sem("o_copied"), sem("o_added"), sem("o_hi_done"), sem("o_lo_done")
        y_summed, y_gated, z_done, stats_done = sem("y_summed"), sem("y_gated"), sem("z_done"), sem("stats_done")
        mv_done, var_done, rstd_done, n_done = sem("mv_done"), sem("var_done"), sem("rstd_done"), sem("n_done")
        scaled, t_done, r_done = sem("scaled3"), sem("t_done"), sem("r_done")
        t_stored, r_stored, aff_stored = sem("t_stored"), sem("r_stored"), sem("aff_stored")
        tt_turned, tt_moved, lg_summed, lg_moved, lg_turned = (sem("tt_turned"), sem("tt_moved"), sem("lg_summed"),
                                                               sem("lg_moved"), sem("lg_turned"))
        lg_maxed, lg_expd, lg_inverted, aff_done = sem("lg_maxed"), sem("lg_expd"), sem("lg_inverted"), sem("aff_done")
        block = ctx.enter_context(nc.Block())

        def run(eng, body, ahead=0):
            for i in range(3):
                body(i)
            with eng.Fori(3, NT - 1) as i:
                body(i)
            for i in range(NT - 1, NT + 3):
                body(i)

        def tile(i):
            return not isinstance(i, int) or 0 <= i < NT

        ORDER = (("S", 0), ("T", 0), ("S", 1), ("T", 1), ("P", 0), ("T", 2), ("P", 1), ("S", 2), ("T", 3),
                 ("P", 2), ("T", 4), ("P", 3), ("S", 3), ("P", 4))

        ORDER_ACT = (("T", 0), ("S", 0), ("T", 1), ("S", 1), ("T", 2), ("T", 3), ("S", 2), ("T", 4), ("S", 3))

        def shift(i, g, steps):
            return i + (g + steps) // G, (g + steps) % G

        @block.sync
        def _(sp):
            mod = scratch["mod"]
            for row, src in ((row_g1, mod[0:1, 2 * d.D:3 * d.D]), (row_tg, io["ln1_g"]), (row_tb, io["ln1_b"]),
                             (row_rg, mod[0:1, 4 * d.D:5 * d.D]), (row_rb, mod[0:1, 3 * d.D:4 * d.D])):
                sp.dma_start(row[:], src.broadcast_to([P, d.D])).then_inc(rows_loaded, 16)
            sp.dma_start(sink[:], io["attn_sink"].broadcast_to([P, d.H])).then_inc(rows_loaded, 16)
            sp.dma_start(router[:], io["moe_router"][0].rearrange("(k p) e -> p k e", p=P)).then_inc(router_loaded, 16)

            def load_qk(i, g):
                qt = scratch["qt"][bass.ds(i, 1), :, g * HG:(g + 1) * HG, :].rearrange("t p h n -> p (t h) n")
                sp.dma_start(q_in[g % 2][:].bitcast(F32), qt).then_inc(qk_loaded[g % 2], 16)
                sp.dma_start(k_in[g % 2][:].bitcast(F32),
                             scratch["kt"][:, g, :, bass.ds(i * P, d.WIN)]).then_inc(qk_loaded[g % 2], 16)

            def load_v(i, g):
                sp.dma_start(v_in[g % 2][:].bitcast(F32), scratch["v"][bass.ds(i, 3), :, g, :]
                             .rearrange("t p n -> p t n")).then_inc(v_loaded[g % 2], 16)

            for g in range(2):
                load_qk(0, g)
                load_v(0, g)

            def body(i):
                for g in range(G):
                    ni, ng = shift(i, g, 2)
                    if tile(i) and tile(ni):
                        sp.wait_ge(scored, 16 * i + HG * (g + 1))
                        load_qk(ni, ng)
                    pi, pg = shift(i, g, -2)
                    if tile(pi) and tile(i):
                        sp.wait_ge(pv_done, KB * (4 * pi + pg + 1))
                        load_v(i, g)
                    t = i - 1
                    if g == 1 and tile(t):
                        wait(sp, z_done, 2 * t)
                        sp.dma_start(x_in[:], io["x"][0, bass.ds(t * P, P), :]).then_inc(x_loaded, 16)
                    t = i - 2
                    if g == 2 and tile(t):
                        sp.wait_ge(t_done, t + 1)
                        sp.dma_start(scratch["tok"][bass.ds(t * P, P), 0:d.D], t_out[:]).then_inc(t_stored, 16)
                    if g == 3 and tile(t):
                        sp.wait_ge(r_done, t + 1)
                        sp.dma_start(scratch["res"][bass.ds(t * P, P), :], r_out[:]).then_inc(r_stored, 16)
                    t = i - 3
                    if g == 3 and tile(t):
                        sp.wait_ge(aff_done, t + 1)
                        sp.dma_start(scratch["tok"][bass.ds(t * P, P), d.D:d.D + d.E],
                                     aff[:, bass.ds(t, 1), :].rearrange("p t e -> p (t e)")).then_inc(aff_stored, 16)
            run(sp, body)
            for s in (t_stored, r_stored, aff_stored):
                sp.wait_ge(s, 16 * NT)

        @block.gpsimd
        def _(pool):
            pool.memset(minus_half[:], -0.5).then_inc(half_made, 1)
            pool.memset(mask[:, 0:2, :], 0.0).then_inc(masks_made, 1)
            pool.memset(mask[:, 2, :], NEG).then_inc(masks_made, 1)
            pool.memset(ones[:], 1.0).then_inc(masks_made, 1)
            pool.wait_ge(masks_made, 1)
            pool.affine_select(out=mask[:, 0, :], in_=mask[:, 0, :], compare_op=ALU.is_ge, fill=NEG, base=0,
                               pattern=[[1, P]], channel_multiplier=-1).then_inc(masks_made, 1)
            pool.affine_select(out=mask[:, 1, :], in_=mask[:, 1, :], compare_op=ALU.is_ge, fill=NEG, base=0,
                               pattern=[[-1, P]], channel_multiplier=1).then_inc(masks_made, 1)
            pool.wait_ge(rows_ready, 1)

            def body(i):
                for g in range(G):
                    pi, pg = shift(i, g, -1)
                    if tile(pi):
                        pool.wait_ge(inverted, 4 * pi + pg + 1)
                        apart(pool, const["carried"])
                        for h in range(HG):
                            last = pool.tensor_scalar(prob[pg][:, h, :], prob[pg][:, h, :],
                                                      inv[pg][:, h:h + 1], 1.0, ALU.mult, ALU.mult)
                        last.then_inc(normed, 1)
                    t = i - 2
                    if g == 0 and tile(t):
                        pool.wait_ge(var_done, t + 1)
                        pool.wait_ge(half_made, 1)
                        pool.tensor_tensor(rstd[:], var_eps[:], minus_half[:], ALU.pow).then_inc(rstd_done, 1)
                    if g == 1 and tile(t):
                        pool.wait_ge(n_done, t + 1)
                        wait(pool, t_stored, 16 * t)
                        wait(pool, tt_turned, 2 * t)
                        pool.tensor_tensor(t_out[:], z[:], row_tg[:], ALU.mult).then_inc(scaled, 1)
                        pool.wait_ge(scaled, 2 * t + 1)
                        pool.tensor_tensor(t_out[:], t_out[:], row_tb[:], ALU.add).then_inc(t_done, 1)
                    if g == 2 and tile(t):
                        wait(pool, r_stored, 16 * t)
                        pool.tensor_tensor(r_out[:], z[:], row_rg[:], ALU.mult).then_inc(scaled, 1)
                        pool.wait_ge(scaled, 2 * t + 2)
                        pool.tensor_tensor(r_out[:], r_out[:], row_rb[:], ALU.add).then_inc(r_done, 1)
            run(pool, body)

        @block.scalar
        def _(act):
            for n in range(4):
                cols = slice(n * BANK // 2, (n + 1) * BANK // 2)
                wait(act, wo_hi_done, n)
                wait(act, wo_lo_done, n)
                act.dma_start(wo_raw[:], io["attn_w_o"][0].rearrange("(k p) n -> p k n", p=P)[:, :, cols]).then_inc(wo_loaded, 16)
                act.wait_ge(wo_loaded, 16 * (n + 1))
                act.activation(wo_hi[:, :, cols], wo_raw[:], ACT.Copy).then_inc(wo_hi_done, 1)

            def exp(i, g, h):
                n = 16 * i + HG * g + h
                if h == 0:
                    wait(act, turned, KB * (4 * (i - 1) + g + 1))
                act.wait_ge(maxed, n + 1)
                act.activation(prob[g][:, h, :], ps_s[h % 2][:, W0:C1 + 1], ACT.Exp,
                               bias=neg_max[g % 2][:, h:h + 1], accum_out=total[g][:, h:h + 1]).then_inc(expd, 1)

            def part(i, g, j):
                m = KB * (4 * i + g) + j
                b = (KB * g + j) % 2
                act.wait_ge(turned, m + 1)
                wait(act, pv_done, m - 1)
                act.activation(pt_hi[b][:], ps_t[b][:], ACT.Copy).then_inc(pt_hi_done, 1)

            def move_tt(t, half):
                act.wait_ge(tt_turned, 2 * t + half + 1)
                if half == 0:
                    wait(act, lg_summed, t)
                act.activation(tt[:, 4 * half:4 * half + 4, :], ps_y[:].rearrange("p (k n) -> p k n", n=P),
                               ACT.Copy).then_inc(tt_moved, 1)

            def body(i):
                for g in range(G):
                    pi, pg = shift(i, g, -2)
                    t = i - 3
                    for what, n in ORDER_ACT:
                        if tile(t) and g == 0 and (what, n) in (("S", 2), ("S", 3)):
                            move_tt(t, n - 2)
                        if tile(t) and g == 1 and (what, n) == ("T", 1):
                            act.wait_ge(lg_summed, t + 1)
                            act.activation(lg_t[:], ps_y[0:d.E, 0:P], ACT.Copy).then_inc(lg_moved, 1)
                        if what == "S" and tile(i):
                            exp(i, g, n)
                        if what == "T" and tile(pi):
                            part(pi, pg, n)
                        if (what, n) == ("T", 1) and g == 2 and tile(i - 1):
                            act.wait_ge(o_added, 4 * i)
                            wait(act, y_summed, 2 * (i - 1))
                            act.activation(o_hi[:], o_sum[:], ACT.Copy).then_inc(o_hi_done, 1)
                    if g == 1 and tile(t):
                        act.wait_ge(lg_maxed, t + 1)
                        act.activation(lg_exp[:], ps_y[:, LG:LG + d.E], ACT.Exp, bias=lg_max[:],
                                       accum_out=lg_sum[:]).then_inc(lg_expd, 1)
                    if tile(pi):
                        m = 4 * pi + pg
                        act.wait_ge(pv_done, KB * (m + 1))
                        wait(act, o_added, m)
                        act.activation(o_low[:], ps_o[d.DH:P], ACT.Copy).then_inc(o_copied, 1)
            run(act, body)

        @block.vector
        def _(dve):
            dve.wait_ge(rows_loaded, 96)
            dve.memset(sink_key[:], 0.0).then_inc(sink_ready, 1)
            for n in range(3):
                dve.tensor_copy(sink_part[n][:], sink[:]).then_inc(sink_ready, 1)
                dve.wait_ge(sink_ready, 3 * n + 2 if n else 2)
                dve.tensor_copy(sink_key[32 * n:32 * n + 1, :], sink_part[n][32 * n:32 * n + 1, :]).then_inc(sink_ready, 1)
                if n < 2:
                    dve.tensor_tensor(sink[:], sink[:], sink_part[n][:], ALU.subtract).then_inc(sink_ready, 1)
                    dve.wait_ge(sink_ready, 3 * n + 4)
            dve.tensor_scalar(row_rg[:], row_rg[:], 1.0, None, ALU.add).then_inc(rows_mid, 1)
            dve.tensor_scalar(z[:], row_tg[:], d.alpha, None, ALU.mult).then_inc(rows_mid, 1)
            dve.tensor_scalar(t_out[:], row_tb[:], d.alpha, None, ALU.mult).then_inc(rows_mid, 1)
            dve.wait_ge(rows_mid, 3)
            dve.tensor_tensor(row_tg[:], row_tg[:], row_rg[:], ALU.mult).then_inc(rows_mid, 1)
            dve.tensor_tensor(row_tb[:], row_tb[:], row_rg[:], ALU.mult).then_inc(rows_mid, 1)
            dve.wait_ge(rows_mid, 5)
            dve.tensor_tensor(row_tb[:], row_tb[:], row_rb[:], ALU.add).then_inc(rows_mid, 1)
            dve.wait_ge(rows_mid, 6)
            dve.tensor_copy(row_rg[:], z[:]).then_inc(rows_mid, 1)
            dve.tensor_copy(row_rb[:], t_out[:]).then_inc(rows_mid, 1)
            dve.wait_ge(rows_mid, 8)
            dve.sem_inc(rows_ready, 1)
            for n in range(4):
                cols = slice(n * BANK // 2, (n + 1) * BANK // 2)
                dve.wait_ge(wo_hi_done, n + 1)
                dve.tensor_tensor(wo_lo[:, :, cols], wo_raw[:], wo_hi[:, :, cols].bitcast(F32),
                                  ALU.subtract).then_inc(wo_lo_done, 1)

            def score_max(i, g, h):
                n = 16 * i + HG * g + h
                dve.wait_ge(scored, n + 1)
                if h == 0:
                    wait(dve, expd, HG * (4 * i + g - 1))
                dve.tensor_reduce(neg_max[g % 2][:, h:h + 1], ps_s[h % 2][:, W0:C1 + 1], AX_X, ALU.max,
                                  negate=True).then_inc(maxed, 1)

            def invert(i, g):
                m = 4 * i + g
                dve.wait_ge(expd, HG * (m + 1))
                wait(dve, normed, m - 3)
                dve.reciprocal(inv[g][:], total[g][:]).then_inc(inverted, 1)

            def part(i, g, j):
                m = KB * (4 * i + g) + j
                b = (KB * g + j) % 2
                dve.wait_ge(pt_hi_done, m + 1)
                wait(dve, pv_done, m - 1)
                dve.tensor_tensor(pt_lo[b][:], ps_t[b][:], pt_hi[b][:].bitcast(F32), ALU.subtract).then_inc(pt_lo_done, 1)

            def join(i, g):
                m = 4 * i + g
                dve.wait_ge(o_copied, m + 1)
                if g == 0:
                    wait(dve, o_lo_done, i)
                for odd in range(2):
                    last = dve.tensor_tensor(o_sum[odd * d.DH:(odd + 1) * d.DH, 2 * g:2 * g + 2, :],
                                             ps_o[0:d.DH, odd:HG:2, :], o_low[:, odd:HG:2, :], ALU.add)
                last.then_inc(o_added, 1)

            def split_o(t):
                dve.wait_ge(o_hi_done, t + 1)
                wait(dve, y_summed, 2 * t)
                dve.tensor_tensor(o_lo[:], o_sum[:], o_hi[:].bitcast(F32), ALU.subtract).then_inc(o_lo_done, 1)

            def normalise(t):
                dve.wait_ge(rstd_done, t + 1)
                dve.tensor_scalar(z[:], z[:], mean_var[:, 0:1], rstd[:], ALU.subtract, ALU.mult).then_inc(n_done, 1)

            def affinities(t):
                dve.wait_ge(lg_expd, t + 1)
                dve.reciprocal(lg_inv[:], lg_sum[:]).then_inc(lg_inverted, 1)
                dve.wait_ge(lg_inverted, t + 1)
                dve.tensor_scalar(aff[:, bass.ds(t, 1), :].rearrange("p t e -> p (t e)"), lg_exp[:], lg_inv[:],
                                  None, ALU.mult).then_inc(aff_done, 1)

            def gate_in(t, half):
                n = 2 * t + half
                cols = slice(half * BANK, (half + 1) * BANK)
                dve.wait_ge(y_summed, n + 1)
                if half == 0:
                    wait(dve, r_done, t)
                dve.tensor_tensor(z[:, cols], ps_y[:], row_g1[:, cols], ALU.mult).then_inc(y_gated, 1)

            def add_in(t, half):
                n = 2 * t + half
                cols = slice(half * BANK, (half + 1) * BANK)
                dve.wait_ge(y_gated, n + 1)
                dve.wait_ge(x_loaded, 16 * (t + 1))
                dve.scalar_tensor_tensor(out=z[:, cols], in0=x_in[:, cols], scalar=d.alpha, in1=z[:, cols],
                                         op0=ALU.mult, op1=ALU.add).then_inc(z_done, 1)
                dve.wait_ge(z_done, n + 1)
                dve.bn_stats(stats[:, half, :], z[:, cols]).then_inc(stats_done, 1)
                if half == 1:
                    dve.wait_ge(stats_done, n + 1)
                    apart(dve, const["carried"])
                    dve.bn_aggr(mean_var[:], stats[:].rearrange("p a b -> p (a b)")).then_inc(mv_done, 1)
                    dve.wait_ge(mv_done, t + 1)
                    dve.tensor_scalar(var_eps[:], mean_var[:, 1:2], d.eps, None, ALU.add).then_inc(var_done, 1)

            def body(i):
                for g in range(G):
                    pi, pg = shift(i, g, -2)
                    for what, n in ORDER:
                        if what == "S" and tile(i):
                            score_max(i, g, n)
                        if what == "T" and tile(pi):
                            part(pi, pg, n)
                        if (what, n) == ("T", 1):
                            if g == 3 and tile(i - 1):
                                gate_in(i - 1, 0)
                            if g == 0 and tile(i - 2):
                                gate_in(i - 2, 1)
                            if g == 1 and tile(i - 2):
                                normalise(i - 2)
                        if (what, n) == ("T", 2) and g == 2 and tile(i - 1):
                            split_o(i - 1)
                        if (what, n) == ("T", 4) and g == 2 and tile(i - 3):
                            affinities(i - 3)
                    if g == 1 and tile(i - 3):
                        dve.wait_ge(lg_turned, i - 2)
                        dve.tensor_reduce(lg_max[:], ps_y[:, LG:LG + d.E], AX_X, ALU.max, negate=True).then_inc(lg_maxed, 1)
                    if tile(i):
                        invert(i, g)
                    if tile(pi):
                        join(pi, pg)
                    if g == 3 and tile(i - 1):
                        add_in(i - 1, 0)
                    if g == 0 and tile(i - 2):
                        add_in(i - 2, 1)
            run(dve, body)

        @block.tensor
        def _(pe):
            pe.wait_ge(masks_made, 5)
            pe.wait_ge(sink_ready, 9)

            def scores(i, g, h):
                n = 16 * i + HG * g + h
                s, q, k = ps_s[h % 2], q_in[g % 2], k_in[g % 2]
                if h == 0:
                    pe.wait_ge(qk_loaded[g % 2], 32 * (2 * i + g // 2 + 1))
                wait(pe, expd, n - 1)
                for part in range(2):
                    pe.matmul(s[:, W0:W1], q[:, h, :], k[:, part, :], start=(part == 0), stop=False)
                left = 2 if isinstance(i, int) and i == 0 else 0
                right = 2 if isinstance(i, int) and i == NT - 1 else 1
                pe.matmul(s[:, W0:W0 + P], const["ident_bf"][:], mask[:, left, :], start=False, stop=False)
                pe.matmul(s[:, W1 - P:W1], const["ident_bf"][:], mask[:, right, :], start=False, stop=True)
                for part in range(2):
                    pe.matmul(s[:, W1:C1], q[:, h, :], k_ctx[:, g, part, :], start=(part == 0), stop=(part == 1))
                column = HG * g + h
                last = pe.matmul(s[:, C1:C1 + 1], ones[:], sink_key[:, column:column + 1], start=True, stop=True)
                last.then_inc(scored, 1)

            def turn(i, g, j):
                m = KB * (4 * i + g) + j
                b = (KB * g + j) % 2
                if j == 0:
                    pe.wait_ge(normed, 4 * i + g + 1)
                wait(pe, pt_lo_done, m - 1)
                for h in range(HG):
                    last = pe.transpose(ps_t[b][:, h, :], prob[g][:, h, j * P:(j + 1) * P], const["ident"][:])
                last.then_inc(turned, 1)

            def product(i, g, j):
                m = KB * (4 * i + g) + j
                b = (KB * g + j) % 2
                if j == 0:
                    pe.wait_ge(v_loaded[g % 2], 16 * (2 * i + g // 2 + 1))
                    wait(pe, o_added, 4 * i + g)
                v = v_in[g % 2][:, j, :] if j < 3 else v_ctx[:, j - 3, g, :]
                pe.wait_ge(pt_hi_done, m + 1)
                pe.matmul(ps_o[:], v, pt_hi[b][:], start=(j == 0), stop=False)
                pe.wait_ge(pt_lo_done, m + 1)
                pe.matmul(ps_o[:], v, pt_lo[b][:], start=False, stop=(j == KB - 1)).then_inc(pv_done, 1)

            def output(t, half):
                cols = slice(half * BANK, (half + 1) * BANK)
                if half == 0:
                    pe.wait_ge(o_lo_done, t + 1)
                    pe.wait_ge(wo_lo_done, 4)
                    wait(pe, lg_expd, t - 1)
                wait(pe, y_gated, 2 * t + half)
                for k in range(HP):
                    for n, (o, w) in enumerate(((o_hi, wo_hi), (o_hi, wo_lo), (o_lo, wo_hi))):
                        last = pe.matmul(ps_y[:], o[:, k, :], w[:, k, cols], start=(k == 0 and n == 0),
                                         stop=(k == HP - 1 and n == 2))
                last.then_inc(y_summed, 1)

            def turn_tokens(t, half):
                if half == 0:
                    pe.wait_ge(t_done, t + 1)
                    wait(pe, lg_expd, t)
                    pe.wait_ge(y_gated, min(2 * t + 4, 2 * NT) if isinstance(t, int) else 2 * t + 4)
                wait(pe, tt_moved, 2 * t + half)
                for k in range(4):
                    cols = slice((4 * half + k) * P, (4 * half + k + 1) * P)
                    last = pe.transpose(ps_y[:, k * P:(k + 1) * P], t_out[:, cols], const["ident"][:])
                last.then_inc(tt_turned, 1)

            def logits(t):
                pe.wait_ge(tt_moved, 2 * t + 2)
                pe.wait_ge(router_loaded, 16)
                for k in range(d.KD):
                    last = pe.matmul(ps_y[0:d.E, 0:P], router[:, k, :], tt[:, k, :], start=(k == 0), stop=(k == d.KD - 1))
                last.then_inc(lg_summed, 1)

            def turn_logits(t):
                pe.wait_ge(lg_moved, t + 1)
                apart(pe, const["carried"])
                pe.transpose(ps_y[:, LG:LG + d.E], lg_t[:], const["ident"][0:d.E, 0:d.E]).then_inc(lg_turned, 1)

            def body(i):
                for g in range(G):
                    pi, pg = shift(i, g, -2)
                    t = i - 3
                    for what, n in ORDER:
                        if tile(t) and g == 0 and (what, n) in (("S", 2), ("S", 3)):
                            turn_tokens(t, n - 2)
                        if tile(t) and g == 1 and (what, n) == ("T", 1):
                            logits(t)
                        if tile(t) and g == 1 and (what, n) == ("S", 2):
                            turn_logits(t)
                        if what == "S" and tile(i):
                            scores(i, g, n)
                        if what == "T" and tile(pi):
                            turn(pi, pg, n)
                        if what == "P" and tile(pi):
                            product(pi, pg, n)
                    if g in (2, 3) and tile(i - 1):
                        output(i - 1, g - 2)
            run(pe, body)



def choice(nc, d, const, aff, slot_of):
    NB = 30
    NE = d.NT * d.E
    with ExitStack() as ctx:
        sb = lambda n, s, t=F32: ctx.enter_context(nc.sbuf_tensor(n, s, t))
        psum = lambda n, s: ctx.enter_context(nc.psum_tensor(n, s, F32))
        sem = lambda n: ctx.enter_context(nc.semaphore(n))
        ones = sb("ones_bf", [P, P], BF16)
        upto = sb("upto_bf", [P, P], BF16)
        bit = sb("bit", [P, 1], I32)
        best = sb("best", [P, d.E])
        cand = sb("cand", [P, d.E])
        kept = sb("kept", [P, d.E])
        reach = sb("reach", [P, d.NT, d.E], BF16)
        count = sb("count", [P, d.E], BF16)
        above = sb("above", [P, d.NT, d.E], BF16)
        equal = sb("equal", [P, d.NT, d.E], BF16)
        missing = sb("missing", [P, d.E])
        early = sb("early", [P, d.NT, d.E])
        chosen = sb("chosen", [P, d.NT, d.E], BF16)
        ps_n = psum("ps_n", [P, BANK])
        ps_r = psum("ps_r", [P, BANK])
        made, started = sem("made4"), sem("started")
        tried, compared, counted, summed, judged, raised, halved = (sem("tried"), sem("compared"), sem("counted"),
                                                                    sem("summed4"), sem("judged"), sem("raised"), sem("halved"))
        masks_done, count_done, above_summed, missing_done = sem("masks_done"), sem("count_done"), sem("above_summed"), sem("missing_done")
        ranked, early_done, chosen_done, placed, slots_mid, slots_done = (sem("ranked"), sem("early_done"), sem("chosen_done"),
                                                                          sem("placed"), sem("slots_mid"), sem("slots_done"))
        block = ctx.enter_context(nc.Block())

        def over_tiles(ap):
            return copies(ap, 1, d.NT)

        @block.gpsimd
        def _(pool):
            pool.memset(ones[:], 1.0).then_inc(made, 1)
            pool.memset(upto[:], 1.0).then_inc(made, 1)
            pool.wait_ge(made, 2)
            pool.affine_select(out=upto[:], in_=upto[:], compare_op=ALU.is_ge, fill=0.0, base=0,
                               pattern=[[1, P]], channel_multiplier=-1).then_inc(made, 1)

        @block.vector
        def _(dve):
            dve.memset(bit[:], 1 << (NB - 1)).then_inc(started, 1)
            dve.memset(best[:], 0.0).then_inc(started, 1)
            dve.wait_ge(started, 2)

            def try_bit(i):
                wait(dve, raised, i)
                wait(dve, halved, i)
                dve.tensor_tensor(cand[:].bitcast(I32), best[:].bitcast(I32), bit[:].broadcast_to([P, d.E]),
                                  ALU.bitwise_or).then_inc(tried, 1)
                dve.wait_ge(tried, i + 1)
                dve.tensor_tensor(reach[:], aff[:], over_tiles(cand[:]), ALU.is_ge).then_inc(compared, 1)
                dve.wait_ge(compared, i + 1)
                with nc.allow_low_precision(reason="counts up to 16 are exact"):
                    dve.tensor_reduce(count[:], reach[:].rearrange("p t e -> p e t"), AX_X, ALU.add).then_inc(counted, 1)
                dve.tensor_scalar(bit[:], bit[:], 1, None, ALU.logical_shift_right).then_inc(halved, 1)
                dve.wait_ge(summed, i + 1)
                dve.scalar_tensor_tensor(out=kept[:], in0=ps_n[:, 0:d.E], scalar=float(d.CAP), in1=cand[:],
                                         op0=ALU.is_ge, op1=ALU.mult).then_inc(judged, 1)
                dve.wait_ge(judged, i + 1)
                dve.tensor_tensor(best[:], best[:], kept[:], ALU.max).then_inc(raised, 1)
            peeled(dve, NB, try_bit)
            dve.wait_ge(raised, NB)
            dve.tensor_tensor(above[:], aff[:], over_tiles(best[:]), ALU.is_gt).then_inc(masks_done, 1)
            dve.tensor_tensor(equal[:], aff[:], over_tiles(best[:]), ALU.is_equal).then_inc(masks_done, 1)
            dve.wait_ge(masks_done, 1)
            with nc.allow_low_precision(reason="counts up to 16 are exact"):
                dve.tensor_reduce(count[:], above[:].rearrange("p t e -> p e t"), AX_X, ALU.add).then_inc(count_done, 1)
            dve.wait_ge(above_summed, 1)
            dve.tensor_scalar(missing[:], ps_n[:, 0:d.E], -1.0, float(d.CAP), ALU.mult, ALU.add).then_inc(missing_done, 1)
            dve.wait_ge(missing_done, 1)
            dve.wait_ge(ranked, 1)
            dve.tensor_tensor(early[:], ps_r[:, 0:NE].rearrange("p (t e) -> p t e", e=d.E), over_tiles(missing[:]),
                              ALU.is_le).then_inc(early_done, 1)
            dve.wait_ge(early_done, 1)
            dve.tensor_tensor(early[:], early[:], equal[:], ALU.mult).then_inc(early_done, 1)
            dve.wait_ge(early_done, 2)
            dve.tensor_tensor(chosen[:], early[:], above[:], ALU.add).then_inc(chosen_done, 1)
            dve.wait_ge(placed, 1)
            dve.tensor_tensor(slot_of[:], ps_r[:, 0:NE].rearrange("p (t e) -> p t e", e=d.E), chosen[:],
                              ALU.mult).then_inc(slots_mid, 1)
            dve.wait_ge(slots_mid, 1)
            dve.tensor_scalar(slot_of[:], slot_of[:], -1.0, None, ALU.add).then_inc(slots_done, 1)

        @block.tensor
        def _(pe):
            def rank(of):
                flat = of[:].rearrange("p t e -> p (t e)")
                for back in range(d.NT):
                    last = pe.matmul(ps_r[:, back * d.E:NE], (ones if back else upto)[:], flat[:, 0:NE - back * d.E],
                                     start=(back == 0), stop=(back == d.NT - 1))
                return last

            pe.wait_ge(made, 3)

            def count_all(i):
                pe.wait_ge(counted, i + 1)
                wait(pe, judged, i)
                pe.matmul(ps_n[:, 0:d.E], ones[:], count[:], start=True, stop=True).then_inc(summed, 1)
            peeled(pe, NB, count_all)
            pe.wait_ge(masks_done, 2)
            rank(equal).then_inc(ranked, 1)
            pe.wait_ge(count_done, 1)
            pe.wait_ge(judged, NB)
            pe.matmul(ps_n[:, 0:d.E], ones[:], count[:], start=True, stop=True).then_inc(above_summed, 1)
            pe.wait_ge(chosen_done, 1)
            rank(chosen).then_inc(placed, 1)



def experts(nc, d, io, scratch, const, slot_of):
    KH = 4
    RAW, RING = 3, 3
    NS = d.CAP // P
    FC = d.F // BANK
    HF = d.F // P
    PIECES = 2 * FC + 2 * (HF // (2 * KH))
    SUBS = 2 * PIECES
    FILLS = 2 * FC + d.KD // 2
    TB = 3
    LAST = d.E - 1

    def pieces():
        w1 = io["moe_w1"][0].rearrange("e (k p) n -> e p k n", p=P)
        w3 = io["moe_w3"][0].rearrange("e (k p) n -> e p k n", p=P)
        w2 = io["moe_w2"][0].rearrange("e (k p) n -> e p k n", p=P)
        for c in range(FC):
            yield w1, 0, c
            yield w3, 0, c
        for c in range(2):
            for k in range(0, HF, 2 * KH):
                yield w2, k, c

    with ExitStack() as ctx:
        sb = lambda n, s, t=F32: ctx.enter_context(nc.sbuf_tensor(n, s, t))
        psum = lambda n, s: ctx.enter_context(nc.psum_tensor(n, s, F32))
        sem = lambda n: ctx.enter_context(nc.semaphore(n))
        raw = [sb(f"raw{b}", [P, 2 * KH, BANK]) for b in range(RAW)]
        w_hi = [sb(f"w_hi{b}", [P, KH, BANK], F32R) for b in range(RING)]
        w_lo = [sb(f"w_lo{b}", [P, KH, BANK], F32R) for b in range(RING)]
        xg = sb("xg", [P, NS, d.D + d.E])
        xt_hi = sb("xt_hi", [P, d.KD, d.CAP], F32R)
        xt_lo = sb("xt_lo", [P, d.KD, d.CAP], F32R)
        gate = sb("gate", [P, NS])
        act_out = sb("act_out", [P, NS, BANK])
        hid = sb("hid", [P, NS, BANK])
        ht_hi = sb("ht_hi", [P, HF, d.CAP], F32R)
        ht_lo = sb("ht_lo", [P, HF, d.CAP], F32R)
        y = sb("y", [P, NS, d.D])
        one_hot = sb("one_hot", [P, d.NT, d.CAP], F16)
        slots = sb("slots", [P, d.CAP], F16)
        slots_i = sb("slots_i", [P, d.CAP], I32)
        token = sb("token", [P, d.NT], F16)
        token_i = sb("token_i", [P, d.NT], I32)
        index = [sb(f"index{s}", [P, 1], U32) for s in range(NS)]
        index_out = [sb(f"index_out{s}", [P, 1], U32) for s in range(NS)]
        row_g2 = sb("row_g2", [P, d.D])
        ps = {"A": psum("ps_a", [P, NS, BANK]), "B": psum("ps_b", [P, NS, BANK])}
        ps_t = [psum(f"ps_et{b}", [P, 2, d.CAP]) for b in range(TB)]
        ps_i = psum("ps_i", [P, BANK])

        raw_loaded = [sem(f"raw_loaded{b}") for b in range(RAW)]
        row_loaded, counted, tables_done = sem("row_loaded"), sem("iotas"), sem("tables_done")
        w_hi_done, w_lo_done, used = sem("ew_hi_done"), sem("ew_lo_done"), sem("used")
        hot, indexed, index_done = sem("hot"), sem("indexed"), sem("index_done")
        gathered, gate_done, scattered = sem("gathered"), sem("gate_done"), sem("scattered")
        index_kept = sem("index_kept")
        turned, hi_done, lo_done = sem("e_turned"), sem("e_hi_done"), sem("e_lo_done")
        activated, hid_done, y_done = sem("activated"), sem("hid_done"), sem("y_done")
        block = ctx.enter_context(nc.Block())

        ACTIVATE = {4 * c + 2: c for c in range(FC)}
        MULTIPLY = {4 * c + 4: c for c in range(FC)}
        TURN = {4 * c + 6: c for c in range(FC - 1)} | {4 * FC + 1: FC - 1}
        INDEX, Y0, TURN_X = 4, 4 * FC + 4, SUBS - 2

        def run(eng, body):
            body(0, True)
            with eng.Fori(1, LAST) as e:
                body(e, True)
            body(LAST, False)

        def convert(eng, e, u, kind):
            n = SUBS * e + u
            b, r = u % RING, (u // 2) % RAW
            src = raw[r][:, (u % 2) * KH:(u % 2 + 1) * KH, :]
            wait(eng, used, n - RING + 1)
            if kind == "hi":
                eng.wait_ge(raw_loaded[r], 16 * ((PIECES // RAW) * e + (u // 2) // RAW + 1))
                eng.activation(w_hi[b][:], src, ACT.Copy).then_inc(w_hi_done, 1)
            else:
                eng.wait_ge(w_hi_done, n + 1)
                eng.tensor_tensor(w_lo[b][:], src, w_hi[b][:].bitcast(F32), ALU.subtract).then_inc(w_lo_done, 1)

        def fills_hid(c):
            return range(2 * c, 2 * c + 2)

        FILLS_X = range(2 * FC, FILLS)

        def split_fill(eng, e, f, kind):
            n = FILLS * e + f + d.KD // 2
            bank = ps_t[(f + d.KD // 2) % TB]
            hi, lo, at = (ht_hi, ht_lo, 2 * f) if f < 2 * FC else (xt_hi, xt_lo, 2 * (f - 2 * FC))
            if kind == "hi":
                eng.wait_ge(turned, n + 1)
                eng.activation(hi[:, at:at + 2, :], bank[:], ACT.Copy).then_inc(hi_done, 1)
            else:
                eng.wait_ge(hi_done, n + 1)
                eng.tensor_tensor(lo[:, at:at + 2, :], bank[:], hi[:, at:at + 2, :].bitcast(F32),
                                  ALU.subtract).then_inc(lo_done, 1)

        @block.sync
        def _(sp):
            sp.dma_start(row_g2[:], scratch["mod"][0:1, 5 * d.D:6 * d.D].broadcast_to([P, d.D])).then_inc(row_loaded, 16)

            def body(e, _):
                for n, (w, k, c) in enumerate(pieces()):
                    wait(sp, w_lo_done, SUBS * e + 2 * (n - RAW) + 2)
                    sp.dma_start(raw[n % RAW][:], w[bass.ds(e, 1), :, k:k + 2 * KH, c * BANK:(c + 1) * BANK]
                                 .rearrange("e p k n -> (e p) k n")).then_inc(raw_loaded[n % RAW], 16)
            run(sp, body)

        @block.gpsimd
        def _(pool):
            pool.iota(slots_i[:], [[1, d.CAP]], base=0, channel_multiplier=0).then_inc(counted, 1)
            pool.iota(token_i[:], [[P, d.NT]], base=0, channel_multiplier=1).then_inc(counted, 1)

            def gather(e):
                pool.wait_ge(index_done, e + 1)
                wait(pool, turned, FILLS * (e - 1) + d.KD // 2)
                wait(pool, gate_done, e)
                apart(pool, const["carried"])
                for s in range(NS):
                    pool.indirect_dma_start(xg[:, s, :], None, scratch["tok"],
                                            bass.IndirectOffsetOnAxis(ap=index[s][:], axis=0)).then_inc(gathered, 16)

            def body(e, more):
                wait(pool, scattered, 16 * NS * e)
                pool.wait_ge(index_done, e + 1)
                apart(pool, const["carried"])
                for s in range(NS):
                    last = pool.tensor_copy(index_out[s][:], index[s][:])
                last.then_inc(index_kept, 1)
                if more:
                    gather(e + 1)
                pool.wait_ge(index_kept, e + 1)
                pool.wait_ge(y_done, 2 * NS * (e + 1))
                apart(pool, const["carried"])
                for s in range(NS):
                    pool.indirect_dma_start(scratch["res"], bass.IndirectOffsetOnAxis(ap=index_out[s][:], axis=0),
                                            y[:, s, :], None, compute_op=ALU.add).then_inc(scattered, 16)
            gather(0)
            run(pool, body)
            pool.wait_ge(scattered, 16 * NS * d.E)

        @block.scalar
        def _(act):
            for u in range(RING):
                convert(act, 0, u, "hi")
            for f in FILLS_X:
                split_fill(act, -1, f, "hi")

            def body(e, more):
                for u in range(SUBS):
                    if u in ACTIVATE:
                        act.wait_ge(used, SUBS * e + u)
                        wait(act, hid_done, FC * e + ACTIVATE[u])
                        act.activation(act_out[:], ps["A"][:], ACT.Silu).then_inc(activated, 1)
                    if u in TURN:
                        for f in fills_hid(TURN[u]):
                            split_fill(act, e, f, "hi")
                    if u == TURN_X and more:
                        for f in FILLS_X:
                            split_fill(act, e, f, "hi")
                    if more or u + RING < SUBS:
                        convert(act, e, u + RING, "hi")
            run(act, body)

        @block.vector
        def _(dve):
            def make_hot(e):
                wait(dve, indexed, e)
                dve.tensor_tensor(one_hot[:], copies(slots[:], 1, d.NT),
                                  slot_of[:, :, bass.ds(e, 1)].broadcast_to([P, d.NT, d.CAP]),
                                  ALU.is_equal).then_inc(hot, 1)

            def take_index(e):
                dve.wait_ge(indexed, e + 1)
                wait(dve, gathered, 16 * NS * e)
                wait(dve, index_kept, e)
                for s in range(NS):
                    last = dve.tensor_copy(index[s][:], ps_i[:, s:s + 1])
                last.then_inc(index_done, 1)

            def weigh(e, c):
                dve.wait_ge(used, SUBS * e + Y0 + 4 * c)
                wait(dve, scattered, 16 * NS * e)
                for s in range(NS):
                    cols = slice(c * BANK, (c + 1) * BANK)
                    dve.scalar_tensor_tensor(out=y[:, s, cols], in0=ps["AB"[c]][:, s, :], scalar=gate[:, s:s + 1],
                                             in1=row_g2[:, cols], op0=ALU.mult, op1=ALU.mult).then_inc(y_done, 1)

            dve.wait_ge(counted, 2)
            dve.tensor_copy(slots[:], slots_i[:]).then_inc(tables_done, 1)
            dve.tensor_copy(token[:], token_i[:]).then_inc(tables_done, 1)
            dve.wait_ge(tables_done, 2)
            dve.wait_ge(row_loaded, 16)
            make_hot(0)
            take_index(0)
            for u in range(RING):
                convert(dve, 0, u, "lo")
            for f in FILLS_X:
                split_fill(dve, -1, f, "lo")

            def body(e, more):
                for u in range(SUBS):
                    if u == 0:
                        if not isinstance(e, int) or e > 0:
                            weigh(e - 1, 1)
                        dve.wait_ge(gathered, 16 * NS * (e + 1))
                        wait(dve, y_done, 2 * NS * e)
                        dve.tensor_copy(gate[:], xg[:, :, bass.ds(d.D + e, 1)].rearrange("p s n -> p (s n)")).then_inc(gate_done, 1)
                    if u == 1 and more:
                        make_hot(e + 1)
                    if u in MULTIPLY:
                        c = MULTIPLY[u]
                        dve.wait_ge(used, SUBS * e + u)
                        dve.wait_ge(activated, FC * e + c + 1)
                        wait(dve, turned, FILLS * e + 2 * c + d.KD // 2)
                        dve.tensor_tensor(hid[:], ps["B"][:], act_out[:], ALU.mult).then_inc(hid_done, 1)
                    if u == INDEX and more:
                        take_index(e + 1)
                    if u in TURN:
                        for f in fills_hid(TURN[u]):
                            split_fill(dve, e, f, "lo")
                    if u == Y0:
                        dve.wait_ge(gate_done, e + 1)
                        weigh(e, 0)
                    if u == TURN_X and more:
                        for f in FILLS_X:
                            split_fill(dve, e, f, "lo")
                    if more or u + RING < SUBS:
                        convert(dve, e, u + RING, "lo")
            run(dve, body)
            weigh(LAST, 1)

        @block.tensor
        def _(pe):
            def find(e):
                pe.wait_ge(hot, e + 1)
                wait(pe, index_done, e)
                for s in range(NS):
                    for t in range(d.NT):
                        last = pe.matmul(ps_i[:, s:s + 1], one_hot[:, t, s * P:(s + 1) * P], token[:, t:t + 1],
                                         start=(t == 0), stop=(t == d.NT - 1))
                last.then_inc(indexed, 1)

            def turn(e, f, source):
                n = FILLS * e + f + d.KD // 2
                bank = ps_t[(f + d.KD // 2) % TB]
                wait(pe, lo_done, n - TB + 1)
                for k in range(2):
                    for s in range(NS):
                        last = pe.transpose(bank[:, k, s * P:(s + 1) * P], source(s, k), const["ident"][:])
                return last.then_inc(turned, 1)

            def turn_x(e):
                pe.wait_ge(gathered, 16 * NS * (e + 2))
                for f in FILLS_X:
                    turn(e, f, lambda s, k: xg[:, s, (2 * (f - 2 * FC) + k) * P:(2 * (f - 2 * FC) + k + 1) * P])

            def turn_hid(e, c):
                pe.wait_ge(hid_done, FC * e + c + 1)
                for f in fills_hid(c):
                    turn(e, f, lambda s, k: hid[:, s, (2 * (f % 2) + k) * P:(2 * (f % 2) + k + 1) * P])

            pe.wait_ge(tables_done, 2)
            find(0)
            turn_x(-1)

            def body(e, more):
                for u in range(SUBS):
                    n = SUBS * e + u
                    b = u % RING
                    if u == INDEX and more:
                        find(e + 1)
                    if u in TURN:
                        turn_hid(e, TURN[u])
                    if u == TURN_X and more:
                        turn_x(e)
                    first = u % 2 == 0 if u < 4 * FC else u % 4 == 0
                    stop = u % 2 == 1 if u < 4 * FC else u % 4 == 3
                    if u < 4 * FC:
                        acc, hi, lo, k0 = ps["AB"[u // 2 % 2]], xt_hi, xt_lo, KH * (u % 2)
                        if u == 0:
                            pe.wait_ge(lo_done, FILLS * e + d.KD // 2)
                            wait(pe, y_done, 2 * NS * (e - 1) + NS)
                        elif u == 2:
                            wait(pe, y_done, 2 * NS * e)
                        elif first:
                            c = u // 4
                            pe.wait_ge(activated if u % 4 == 0 else hid_done, FC * e + c)
                    else:
                        c, k0 = (u - 4 * FC) // 4, KH * (u % 4)
                        acc, hi, lo = ps["AB"[c]], ht_hi, ht_lo
                        if first:
                            pe.wait_ge(hid_done, FC * (e + 1))
                            pe.wait_ge(activated, FC * (e + 1))
                        pe.wait_ge(lo_done, FILLS * e + d.KD // 2 + min(2 * (u % 4) + 2, 2 * FC))
                    pe.wait_ge(w_hi_done, n + 1)
                    pe.wait_ge(w_lo_done, n + 1)
                    for k in range(KH):
                        for s in range(NS):
                            rows = slice(s * P, (s + 1) * P)
                            for i, (x, w) in enumerate(((hi, w_hi), (hi, w_lo), (lo, w_hi))):
                                last = pe.matmul(acc[:, s, :], x[:, k0 + k, rows], w[b][:, k, :],
                                                 start=(first and k == 0 and i == 0), stop=(stop and k == KH - 1 and i == 2))
                    last.then_inc(used, 1)
            run(pe, body)



def final_norm(nc, d, io, scratch, const, out):
    NG = 4
    TG = d.NT // NG
    with ExitStack() as ctx:
        sb = lambda n, s, t=F32: ctx.enter_context(nc.sbuf_tensor(n, s, t))
        sem = lambda n: ctx.enter_context(nc.semaphore(n))
        r = sb("r_in", [P, d.NT, d.D])
        row_g = sb("row_g", [P, d.D])
        row_b = sb("row_b", [P, d.D])
        stats = [sb(f"stats6_{b}", [P, 2, 6]) for b in range(2)]
        mean_var = [sb(f"mean_var6_{b}", [P, 2]) for b in range(2)]
        var_eps = sb("var_eps6", [P, d.NT])
        rstd = sb("rstd6", [P, d.NT])
        shift = sb("shift6", [P, d.NT])
        minus_half = sb("minus_half6", [P, 1])
        rows_loaded, half_made = sem("rows_loaded6"), sem("half_made6")
        loaded = [sem(f"r_loaded{q}") for q in range(NG)]
        stats_done, mv_done, var_done, rstd_done, shift_done = (sem("stats_done6"), sem("mv_done6"), sem("var_done6"),
                                                                sem("rstd_done6"), sem("shift_done6"))
        norm_done, gain_done, out_done, stored = sem("norm_done6"), sem("gain_done6"), sem("out_done6"), sem("stored6")
        block = ctx.enter_context(nc.Block())

        def run(eng, step, before=None):
            for q in range(NG):
                if before:
                    before(q)
                with eng.Fori(0, TG // 2) as j:
                    for b in range(2):
                        step(q * TG + 2 * j + b, b)

        def tile_of(ap, t):
            return ap[:, bass.ds(t, 1), :].rearrange("p t n -> p (t n)")

        @block.sync
        def _(sp):
            sp.dma_start(r[:, 0:TG, :], scratch["res"][0:TG * P, :].rearrange("(t p) n -> p t n", p=P)).then_inc(loaded[0], 16)
            for row, src in ((row_g, io["ln2_g"]), (row_b, io["ln2_b"])):
                sp.dma_start(row[:], src.broadcast_to([P, d.D])).then_inc(rows_loaded, 16)
            for q in range(1, NG):
                sp.dma_start(r[:, q * TG:(q + 1) * TG, :], scratch["res"][q * TG * P:(q + 1) * TG * P, :]
                             .rearrange("(t p) n -> p t n", p=P)).then_inc(loaded[q], 16)

            def step(t, b):
                sp.wait_ge(out_done, t + 1)
                sp.dma_start(out[0, bass.ds(t * P, P), :], tile_of(r, t)).then_inc(stored, 16)
            run(sp, step)
            sp.wait_ge(stored, 16 * d.NT)

        @block.gpsimd
        def _(pool):
            pool.memset(minus_half[:], -0.5).then_inc(half_made, 1)
            pool.wait_ge(half_made, 1)
            pool.wait_ge(rows_loaded, 32)

            def step(t, b):
                pool.wait_ge(var_done, t + 1)
                pool.tensor_tensor(rstd[:, bass.ds(t, 1)], var_eps[:, bass.ds(t, 1)], minus_half[:], ALU.pow).then_inc(rstd_done, 1)
                pool.wait_ge(gain_done, t + 1)
                pool.tensor_tensor(tile_of(r, t), tile_of(r, t), row_b[:], ALU.add).then_inc(out_done, 1)
            run(pool, step)

        @block.scalar
        def _(act):
            def step(t, b):
                act.wait_ge(shift_done, t + 1)
                act.activation(tile_of(r, t), tile_of(r, t), ACT.Identity, scale=rstd[:, bass.ds(t, 1)],
                               bias=shift[:, bass.ds(t, 1)]).then_inc(norm_done, 1)
            run(act, step)

        @block.vector
        def _(dve):
            dve.wait_ge(rows_loaded, 32)

            def step(t, b):
                one = bass.ds(t, 1)
                for half in range(2):
                    last = dve.bn_stats(stats[b][:, half, :], r[:, one, half * BANK:(half + 1) * BANK].rearrange("p t n -> p (t n)"))
                last.then_inc(stats_done, 1)
                dve.wait_ge(stats_done, t + 1)
                apart(dve, const["carried"])
                dve.bn_aggr(mean_var[b][:], stats[b][:].rearrange("p a b -> p (a b)")).then_inc(mv_done, 1)
                dve.wait_ge(mv_done, t + 1)
                dve.tensor_scalar(var_eps[:, one], mean_var[b][:, 1:2], d.eps, None, ALU.add).then_inc(var_done, 1)
                dve.wait_ge(rstd_done, t + 1)
                dve.scalar_tensor_tensor(out=shift[:, one], in0=mean_var[b][:, 0:1], scalar=-1.0, in1=rstd[:, one],
                                         op0=ALU.mult, op1=ALU.mult).then_inc(shift_done, 1)
                dve.wait_ge(norm_done, t + 1)
                dve.tensor_tensor(tile_of(r, t), tile_of(r, t), row_g[:], ALU.mult).then_inc(gain_done, 1)
            run(dve, step, lambda q: dve.wait_ge(loaded[q], 16))


def trunk(nc, io, out, stop_after=9):
    d = Dims(*[io[k] for k in ("x", "ctx", "ada_w", "attn_w_qkv", "attn_sink", "moe_router", "moe_w1")])
    scratch = {
        "mod": nc.dram_tensor("mod_scr", (2, d.MOD), F32).ap(),
        "qt": nc.dram_tensor("qt_scr", (d.NT, P, d.H, P), F32).ap(),
        "kt": nc.dram_tensor("kt_scr", (P, d.G, 2, (d.NT + 2) * P), F32).ap(),
        "tok": nc.dram_tensor("tok_scr", (d.T, d.D + d.E), F32).ap(),
        "res": nc.dram_tensor("res_scr", (d.T, d.D), F32).ap(),
        "v": nc.dram_tensor("v_scr", (d.NT + 2, P, d.G, 2 * d.DH), F32).ap(),
    }
    with ExitStack() as ctx:
        sb = lambda n, s, t=F32: ctx.enter_context(nc.sbuf_tensor(n, s, t))
        const = {"ident": sb("ident", [P, P]), "ident_bf": sb("ident_bf", [P, P], BF16),
                 "carried": ctx.enter_context(nc.semaphore("carried"))}
        k_ctx = sb("k_ctx", [P, d.G, 2, d.CTX], F32R)
        v_ctx = sb("v_ctx", [P, d.NC, d.G, 2 * d.DH], F32R)
        aff = sb("aff", [P, d.NT, d.E])
        made = ctx.enter_context(nc.semaphore("made"))
        with nc.Block() as block:
            @block.gpsimd
            def _(pool):
                pool.memset(const["ident"][:], 0.0).then_inc(made, 1)
                pool.memset(const["ident_bf"][:], 0.0).then_inc(made, 1)
                pool.wait_ge(made, 2)
                for m in (const["ident"], const["ident_bf"]):
                    pool.affine_select(out=m[:], in_=m[:], compare_op=ALU.not_equal, fill=1.0, base=0,
                                       pattern=[[-1, P]], channel_multiplier=1)
        with ExitStack() as weights:
            wqkv_hi = weights.enter_context(nc.sbuf_tensor("wqkv_hi", [P, d.KD, d.QKV], F32R))
            wqkv_lo = weights.enter_context(nc.sbuf_tensor("wqkv_lo", [P, d.KD, d.QKV], F32R))
            modulation(nc, d, io, scratch, const, wqkv_hi, wqkv_lo)
            projection(nc, d, io, scratch, const, wqkv_hi, wqkv_lo, k_ctx, v_ctx)
        if stop_after > 2:
            attention(nc, d, io, scratch, const, k_ctx, v_ctx, aff)
        slot_of = sb("slot_of", [P, d.NT, d.E])
        if stop_after > 3:
            choice(nc, d, const, aff, slot_of)
        if stop_after > 4:
            experts(nc, d, io, scratch, const, slot_of)
        if stop_after > 5:
            final_norm(nc, d, io, scratch, const, out)



_INS = ["x", "c", "ctx", "c_ctx", "ada_w", "ada_b", "ln1_g", "ln1_b", "ln2_g", "ln2_b",
        "attn_w_qkv", "attn_sink", "attn_w_o", "moe_router", "moe_w1", "moe_w3", "moe_w2"]


def rotary_tables(tokens, head_dim, grid_w=64, base=10000.0):
    import numpy as np

    pos = np.arange(tokens)
    inv = (np.float32(base) ** (-np.arange(head_dim // 4, dtype=np.float32) / np.float32(head_dim // 4))).astype(np.float32)
    ang = np.concatenate([(pos // grid_w).astype(np.float32)[:, None] * inv,
                          (pos % grid_w).astype(np.float32)[:, None] * inv], axis=1)
    cos, sin = np.cos(ang), np.sin(ang)
    return np.concatenate([cos, cos], 1), np.concatenate([-sin, sin], 1)


def kernel(**inputs):
    import numpy as np
    import concourse.bacc as bacc
    from concourse.bass_utils import run_bass_kernel_spmd

    arrays = {name: np.ascontiguousarray(inputs[name]) for name in _INS}
    shape = arrays["x"].shape
    head_dim = shape[2] // arrays["attn_sink"].shape[1]
    arrays["cos"], arrays["sin"] = rotary_tables(shape[1], head_dim)
    nc = bacc.Bacc("TRN2", target_bir_lowering=False, num_devices=1)
    io = {name: nc.dram_tensor(f"in_{name}", a.shape, mybir.dt.from_np(a.dtype), kind="ExternalInput").ap()
          for name, a in arrays.items()}
    out = nc.dram_tensor("out_x", shape, F32, kind="ExternalOutput").ap()
    trunk(nc, io, out)
    r = run_bass_kernel_spmd(nc, [{f"in_{name}": a for name, a in arrays.items()}], core_ids=[0])
    return r.results[0]["out_x"]
```

```python
from contextlib import ExitStack

import concourse.bass as bass
from concourse import mybir

F32 = mybir.dt.float32
F32R = mybir.dt.float32r
BF16 = mybir.dt.bfloat16
F16 = mybir.dt.float16
U32 = mybir.dt.uint32
I32 = mybir.dt.int32
ALU = mybir.AluOpType
ACT = mybir.ActivationFunctionType
AX_X = mybir.AxisListType.X

P = 128
BANK = 512
NEG = -1e30


class Dims:

    def __init__(self, x, ctx, ada_w, attn_w_qkv, attn_sink, moe_router, moe_w1):
        _, self.T, self.D = x.shape
        self.CTX = ctx.shape[1]
        self.H = attn_sink.shape[1]
        self.DH = self.D // self.H
        self.QKV = attn_w_qkv.shape[2]
        self.G = (self.QKV // self.DH - self.H) // 2
        self.HG = self.H // self.G
        self.E = moe_router.shape[2]
        self.F = moe_w1.shape[3]
        self.CAP = 2 * self.T // self.E
        self.NT = self.T // P
        self.NC = self.CTX // P
        self.KD = self.D // P
        self.MOD = ada_w.shape[2]
        self.WIN = 3 * P
        self.alpha = 2.0 ** 0.25
        self.eps = 1e-5
        assert self.DH == 64 and self.G == 4 and self.HG == 4 and self.QKV == 3 * BANK
        assert self.D == 2 * BANK and self.CTX == 2 * P and self.CAP == 2 * P and self.F == 4 * BANK


def wait(eng, sem, value):
    if isinstance(value, int) and value <= 0:
        return
    eng.wait_ge(sem, value)


def apart(eng, carried):
    eng.sem_inc(carried, 1)


def peeled(eng, n, body):
    body(0)
    with eng.Fori(1, n) as i:
        body(i)


def copies(ap, dim, n):
    shape = list(ap.shape)
    return ap.unsqueeze(dim).broadcast_to(shape[:dim] + [n] + shape[dim:])



def modulation(nc, d, io, scratch, const, wqkv_hi, wqkv_lo):
    NCH = 2 * d.D // BANK
    RING = 3
    WC = BANK // 2
    ada = io["ada_w"][0].rearrange("(p k) n -> p k n", k=d.KD)
    wq = io["attn_w_qkv"][0].rearrange("(k p) n -> p k n", p=P)
    c_act = const["c_act"]
    with ExitStack() as ctx:
        sb = lambda n, s, t=F32: ctx.enter_context(nc.sbuf_tensor(n, s, t))
        sem = lambda n: ctx.enter_context(nc.semaphore(n))
        c_in = sb("c_in", [P, 2, d.KD])
        ada_raw = [sb(f"ada_raw{b}", [P, d.KD, BANK]) for b in range(RING)]
        bias = sb("bias", [2, 2 * d.D])
        mod = sb("mod", [2, 2 * d.D])
        w_raw = [sb(f"w_raw{b}", [P, d.KD, WC]) for b in range(2)]
        ps = [ctx.enter_context(nc.psum_tensor(f"mod_ps{n}", [P, BANK], F32)) for n in range(NCH)]
        c_loaded, c_ready, bias_loaded = sem("c_loaded"), sem("c_ready"), sem("bias_loaded")
        ada_loaded = [sem(f"ada_loaded{n}") for n in range(NCH)]
        mod_summed, mod_ready, mod_stored = sem("mod_summed"), sem("mod_ready"), sem("mod_stored")
        w_loaded = [sem(f"w_loaded{b}") for b in range(2)]
        tables_loaded = sem("tables_loaded")
        w_hi_done, w_lo_done = sem("w_hi_done"), sem("w_lo_done")
        block = ctx.enter_context(nc.Block())

        @block.sync
        def _(sp):
            sp.dma_start(c_in[:, 0, :], io["c"][0].rearrange("(p k) -> p k", k=d.KD)).then_inc(c_loaded, 16)
            sp.dma_start(c_in[:, 1, :], io["c_ctx"].rearrange("(p k) -> p k", k=d.KD)).then_inc(c_loaded, 16)
            sp.dma_start(bias[:], io["ada_b"][0:1, 0:2 * d.D].broadcast_to([2, 2 * d.D])).then_inc(bias_loaded, 16)
            for n in range(NCH):
                wait(sp, mod_summed, n - RING + 1)
                sp.dma_start(ada_raw[n % RING][:], ada[:, :, n * BANK:(n + 1) * BANK]).then_inc(ada_loaded[n], 16)
            sp.wait_ge(mod_ready, NCH)
            sp.dma_start(scratch["mod"][:, 0:2 * d.D], mod[:]).then_inc(mod_stored, 16)
            sp.wait_ge(mod_stored, 16)

        @block.scalar
        def _(act):
            def load(n):
                wait(act, w_lo_done, n - 1)
                act.dma_start(w_raw[n % 2][:], wq[:, :, n * WC:(n + 1) * WC]).then_inc(w_loaded[n % 2], 16)

            load(0)
            load(1)
            act.wait_ge(c_loaded, 32)
            act.activation(c_act[:], c_in[:], ACT.Silu).then_inc(c_ready, 1)
            for n in range(d.QKV // WC):
                act.wait_ge(w_loaded[n % 2], 16 * (n // 2 + 1))
                act.activation(wqkv_hi[:, :, n * WC:(n + 1) * WC], w_raw[n % 2][:], ACT.Copy).then_inc(w_hi_done, 1)
                if n + 2 < d.QKV // WC:
                    load(n + 2)
                if n == 1:
                    for table in ("cos", "sin"):
                        act.dma_start(const[table][:], io[table].rearrange("(t p) h -> p t h", p=P)).then_inc(tables_loaded, 16)
            act.wait_ge(tables_loaded, 32)

        @block.tensor
        def _(pe):
            pe.wait_ge(c_ready, 1)
            for n in range(NCH):
                pe.wait_ge(ada_loaded[n], 16)
                for k in range(d.KD):
                    last = pe.matmul(ps[n][0:2, :], c_act[:, :, k], ada_raw[n % RING][:, k, :], start=(k == 0), stop=(k == d.KD - 1))
                last.then_inc(mod_summed, 1)

        @block.vector
        def _(dve):
            dve.wait_ge(bias_loaded, 16)
            for n in range(d.QKV // WC):
                dve.wait_ge(w_hi_done, n + 1)
                cols = slice(n * WC, (n + 1) * WC)
                dve.tensor_tensor(wqkv_lo[:, :, cols], w_raw[n % 2][:], wqkv_hi[:, :, cols].bitcast(F32),
                                  ALU.subtract).then_inc(w_lo_done, 1)
                if n >= 2:
                    m = n - 2
                    dve.wait_ge(mod_summed, m + 1)
                    cols = slice(m * BANK, (m + 1) * BANK)
                    dve.tensor_tensor(mod[:, cols], ps[m][0:2, :], bias[:, cols], ALU.add).then_inc(mod_ready, 1)



def projection(nc, d, io, scratch, const, wqkv_hi, wqkv_lo, k_ctx, v_ctx):
    S0, S1 = d.NC, d.NC + d.NT
    HK = d.H + d.G
    ROT = HK * d.DH
    HALF = d.DH // 2
    FILL = 4
    NB = 2
    NBLK = d.QKV // BANK
    MC = 4 * d.D // d.NT
    ada = io["ada_w"][0].rearrange("(p k) n -> p k n", k=d.KD)

    def fills_before(s):
        return 2 * s if isinstance(s, int) and s <= S0 else 2 * S0 + 6 * (s - S0)

    def blocks_before(s):
        return s if isinstance(s, int) and s <= S0 else S0 + NBLK * (s - S0)

    with ExitStack() as ctx:
        sb = lambda n, s, t=F32: ctx.enter_context(nc.sbuf_tensor(n, s, t))
        psum = lambda n, s: ctx.enter_context(nc.psum_tensor(n, s, F32))
        sem = lambda n: ctx.enter_context(nc.semaphore(n))
        rows = sb("mod_rows", [P, 4, d.D])
        x_in = [sb(f"x_in{b}", [P, d.D]) for b in range(2)]
        u_hi = [sb(f"u_hi{b}", [P, d.KD, P], F32R) for b in range(2)]
        u_lo = [sb(f"u_lo{b}", [P, d.KD, P], F32R) for b in range(2)]
        cos, sin = const["cos"], const["sin"]
        rot_a = sb("rot_a", [P, HK, d.DH])
        rot_b = sb("rot_b", [P, HK, d.DH])
        q_split = sb("q_split", [P, d.H, 2, d.DH], F32R)
        k_split = sb("k_split", [P, d.G, 2, 2, d.DH], F32R)
        v_split = sb("v_split", [P, d.G, 2, d.DH], F32R)
        qt_out = sb("qt_out", [P, d.H, P])
        kt_out = sb("kt_out", [P, d.G, 2, P])
        ada_raw = sb("ada_raw", [P, d.KD, MC])
        ada_sum = sb("ada_sum", [P, MC])
        mod_bias = sb("mod_bias", [1, MC])
        mod_out = sb("mod_out", [1, MC])
        ps_m = psum("ps_m", [P, BANK])
        ps_x = psum("ps_x", [P, d.KD, P])
        ps_q = psum("ps_q", [P, d.QKV])
        ps_t = [psum(f"ps_t{b}", [P, FILL, P]) for b in range(NB)]
        rows_loaded, rows_ready = sem("rows_loaded"), sem("rows_ready")
        x_loaded = [sem(f"x_loaded{b}") for b in range(2)]
        scaled, modulated = sem("scaled"), sem("modulated")
        x_turned, u_hi_done, u_lo_done = sem("x_turned"), sem("u_hi_done"), sem("u_lo_done")
        projected, rotated, added = sem("projected"), sem("rotated"), sem("added")
        v_hi_done, v_lo_done = sem("v_hi_done"), sem("v_lo_done")
        hi_done, lo_done = sem("hi_done"), sem("lo_done")
        turned, moved = sem("turned"), sem("moved")
        q_stored, k_stored, v_stored = sem("q_stored"), sem("k_stored"), sem("v_stored")
        ada_loaded, ada_added, mod_summed = sem("ada_loaded"), sem("ada_added"), sem("mod_summed2")
        mod_ready, mod_stored = sem("mod_ready2"), sem("mod_stored2")
        zeroed, pads_stored = sem("zeroed"), sem("pads_stored")
        block = ctx.enter_context(nc.Block())

        def run(eng, step, ahead=0):
            for s in range(S0 + 2):
                step(s, s % 2)
            with eng.Fori(0, (d.NT - 2) // 2 - ahead) as j:
                for b in range(2):
                    step(S0 + 2 + 2 * j + b, b)
            for s in range(S1 - 2 * ahead, S1 + 2):
                step(s, s % 2)

        def is_latent(s):
            return not isinstance(s, int) or s >= S0

        def in_range(s):
            return not isinstance(s, int) or 0 <= s < S1

        def fill_plan(s):
            ks = [(False, 0), (False, 2)]
            return ks + [(True, h) for h in range(0, d.H, FILL)] if is_latent(s) else ks

        def blocks(s):
            return range(NBLK) if is_latent(s) else (NBLK - 1,)

        def block_count(s, n):
            return blocks_before(s) + (n + 1 if is_latent(s) else 1)

        def heads_of(n):
            return slice(n * BANK // d.DH, min((n + 1) * BANK // d.DH, HK))

        def fills(s, n):
            plan = list(enumerate(fill_plan(s)))
            return plan[n * len(plan) // NBLK:(n + 1) * len(plan) // NBLK]

        def bank_of(s, f):
            before = fills_before(s) if isinstance(s, int) else fills_before(S0)
            return (before + f) % NB

        @block.sync
        def _(sp):
            def load(s, b):
                wait(sp, x_turned, s - 1)
                src = io["x"][0, bass.ds((s - S0) * P, P), :] if is_latent(s) else io["ctx"][0, s * P:(s + 1) * P, :]
                sp.dma_start(x_in[b][:], src).then_inc(x_loaded[b], 16)

            load(0, 0)
            for r, (stream, part) in enumerate([(0, 1), (0, 0), (1, 1), (1, 0)]):
                sp.dma_start(rows[:, r, :], scratch["mod"][stream:stream + 1, part * d.D:(part + 1) * d.D]
                             .broadcast_to([P, d.D])).then_inc(rows_loaded, 16)

            def load_ada(n):
                wait(sp, ada_added, d.KD * n)
                wait(sp, mod_ready, n)
                cols = bass.ds(2 * d.D + n * MC, MC)
                sp.dma_start(ada_raw[:], ada[:, :, cols]).then_inc(ada_loaded, 16)
                sp.dma_start(mod_bias[:], io["ada_b"][0:1, cols]).then_inc(ada_loaded, 16)

            def store_mod(n):
                sp.wait_ge(mod_ready, n + 1)
                sp.dma_start(scratch["mod"][0:1, bass.ds(2 * d.D + n * MC, MC)], mod_out[:]).then_inc(mod_stored, 16)

            def step(s, b):
                if in_range(s + 1):
                    load(s + 1, 1 - b)
                if in_range(s - 2) and is_latent(s - 2):
                    store_mod(s - 2 - S0)
                if in_range(s - 1) and is_latent(s - 1):
                    load_ada(s - 1 - S0)
                t = s - 2
                if in_range(t) and is_latent(t):
                    lt = t - S0
                    sp.wait_ge(v_hi_done, t + 1)
                    sp.wait_ge(v_lo_done, t + 1)
                    sp.dma_start(scratch["v"][bass.ds(lt + 1, 1)].rearrange("t p g n -> (t p) g n"),
                                 v_split[:].rearrange("p g s n -> p g (s n)").bitcast(F32)).then_inc(v_stored, 16)
                    sp.wait_ge(moved, fills_before(t) + 2)
                    sp.dma_start(scratch["kt"][:, :, :, bass.ds((lt + 1) * P, P)], kt_out[:]).then_inc(k_stored, 16)
                    sp.wait_ge(moved, fills_before(t) + 6)
                    sp.dma_start(scratch["qt"][bass.ds(lt, 1)].rearrange("t p h n -> (t p) h n"),
                                 qt_out[:]).then_inc(q_stored, 16)
            run(sp, step, ahead=1)
            sp.wait_ge(pads_stored, 64)
            for s in (q_stored, k_stored, v_stored, mod_stored):
                sp.wait_ge(s, 16 * d.NT)

        @block.gpsimd
        def _(pool):
            pool.wait_ge(rows_ready, 1)

            def modulate(s, b):
                r = 0 if is_latent(s) else 2
                pool.wait_ge(x_loaded[b], 16 * ((s - b) // 2 + 1) if isinstance(s, int) else
                             16 * (S0 // 2 + 1) + 8 * (s - S0 - b))
                pool.tensor_tensor(x_in[b][:], x_in[b][:], rows[:, r, :], ALU.mult).then_inc(scaled, 1)
                pool.wait_ge(scaled, s + 1)
                pool.tensor_tensor(x_in[b][:], x_in[b][:], rows[:, r + 1, :], ALU.add).then_inc(modulated, 1)

            modulate(0, 0)

            def step(s, b):
                t = s - 1
                for n in range(NBLK):
                    if in_range(t) and is_latent(t):
                        pool.wait_ge(rotated, block_count(t, n))
                        heads = heads_of(n)
                        pool.tensor_tensor(rot_a[:, heads, :], rot_a[:, heads, :], rot_b[:, heads, :],
                                           ALU.add).then_inc(added, 1)
                    elif in_range(t) and n in blocks(t):
                        pool.wait_ge(rotated, block_count(t, n))
                        pool.sem_inc(added, 1)
                    if n == 0 and in_range(s + 1):
                        modulate(s + 1, 1 - b)
            run(pool, step, ahead=1)

        @block.scalar
        def _(act):
            act.wait_ge(zeroed, 1)
            for t in (0, d.NT + 1):
                act.dma_start(scratch["kt"][:, :, :, t * P:(t + 1) * P],
                             qt_out[:, 0:2 * d.G, :].rearrange("p (g s) n -> p g s n", s=2)).then_inc(pads_stored, 16)
                act.dma_start(scratch["v"][t], qt_out[:, 0:d.G, :]).then_inc(pads_stored, 16)

            def split_hi(t):
                act.wait_ge(added, blocks_before(t + 1))
                wait(act, turned, fills_before(t))
                if is_latent(t):
                    act.activation(q_split[:, :, 0, :], rot_a[:, 0:d.H, :], ACT.Copy)
                act.activation(k_split[:, :, 0, :, :], copies(rot_a[:, d.H:HK, :], 2, 2),
                               ACT.Copy).then_inc(hi_done, 1)

            def move(t, n):
                for f, (is_q, h) in fills(t, n):
                    bank = ps_t[bank_of(t, f)]
                    act.wait_ge(turned, fills_before(t) + f + 1)
                    if is_latent(t):
                        wait(act, q_stored if is_q else k_stored, 16 * (t - S0))
                        act.wait_ge(pads_stored, 64)
                    if is_q:
                        dst, src = qt_out[:, h:h + FILL, :], bank[:]
                    else:
                        src = bank[:].rearrange("p (g s) n -> p g s n", s=2)
                        dst = kt_out[:, h:h + 2] if is_latent(t) else k_ctx[:, h:h + 2, :, t * P:(t + 1) * P]
                    act.activation(dst, src, ACT.Copy, scale=d.DH ** -0.5 if is_q else 1.0).then_inc(moved, 1)

            def split_v_hi(t):
                act.wait_ge(rotated, blocks_before(t + 1))
                if is_latent(t):
                    wait(act, v_stored, 16 * (t - S0))
                    v_hi = v_split[:, :, 0, :]
                else:
                    v_hi = v_ctx[:, t, :, 0:d.DH]
                act.activation(v_hi, ps_q[:, ROT:d.QKV].rearrange("p (g n) -> p g n", g=d.G),
                               ACT.Copy).then_inc(v_hi_done, 1)

            def step(s, b):
                if in_range(s - 2):
                    split_hi(s - 2)
                if in_range(s):
                    act.wait_ge(x_turned, s + 1)
                    wait(act, projected, blocks_before(s - 1))
                    act.activation(u_hi[b][:], ps_x[:], ACT.Copy).then_inc(u_hi_done, 1)
                if in_range(s - 2):
                    move(s - 2, 0)
                    move(s - 2, 1)
                if in_range(s - 1):
                    split_v_hi(s - 1)
                if in_range(s - 2):
                    move(s - 2, 2)
            run(act, step)

        @block.vector
        def _(dve):
            dve.memset(qt_out[:, 0:2 * d.G, :], 0.0).then_inc(zeroed, 1)
            dve.wait_ge(rows_loaded, 64)
            dve.tensor_scalar(rows[:, 0:4:2, :], rows[:, 0:4:2, :], 1.0, None, ALU.add).then_inc(rows_ready, 1)

            def split_lo(t):
                dve.wait_ge(hi_done, t + 1)
                wait(dve, turned, fills_before(t))
                if is_latent(t):
                    dve.tensor_tensor(q_split[:, :, 1, :], rot_a[:, 0:d.H, :],
                                      q_split[:, :, 0, :].bitcast(F32), ALU.subtract)
                dve.tensor_tensor(k_split[:, :, 1, :, :], copies(rot_a[:, d.H:HK, :], 2, 2),
                                  k_split[:, :, 0, :, :].bitcast(F32), ALU.subtract).then_inc(lo_done, 1)

            def rotate(t, n):
                dve.wait_ge(projected, block_count(t, n))
                wait(dve, hi_done, t)
                wait(dve, lo_done, t)
                heads = heads_of(n)
                count = heads.stop - heads.start
                src = ps_q[:, heads.start * d.DH:heads.stop * d.DH].rearrange("p (h n) -> p h n", n=d.DH)
                if is_latent(t):
                    wait(dve, added, blocks_before(t))
                    cs = cos[:, bass.ds(t - S0, 1), :].broadcast_to([P, count, d.DH])
                    dve.tensor_tensor(rot_a[:, heads, :], src, cs, ALU.mult)
                    for to, of in ((0, 1), (1, 0)):
                        sn = sin[:, bass.ds(t - S0, 1), to * HALF:(to + 1) * HALF].broadcast_to([P, count, HALF])
                        last = dve.tensor_tensor(rot_b[:, heads, to * HALF:(to + 1) * HALF],
                                                 src[:, :, of * HALF:(of + 1) * HALF], sn, ALU.mult)
                    last.then_inc(rotated, 1)
                else:
                    dve.tensor_copy(rot_a[:, heads, :], src).then_inc(rotated, 1)

            def split_v_lo(t):
                dve.wait_ge(v_hi_done, t + 1)
                if is_latent(t):
                    v_hi, v_lo = v_split[:, :, 0, :], v_split[:, :, 1, :]
                    wait(dve, v_stored, 16 * (t - S0))
                else:
                    v_hi, v_lo = v_ctx[:, t, :, 0:d.DH], v_ctx[:, t, :, d.DH:2 * d.DH]
                dve.tensor_tensor(v_lo, ps_q[:, ROT:d.QKV].rearrange("p (g n) -> p g n", g=d.G),
                                  v_hi.bitcast(F32), ALU.subtract).then_inc(v_lo_done, 1)

            def add_ada(n):
                dve.wait_ge(ada_loaded, 32 * (n + 1))
                dve.tensor_scalar(ada_sum[:], ada_raw[:, 0, :], const["c_act"][:, 0, 0:1], None, ALU.mult).then_inc(ada_added, 1)
                for k in range(1, d.KD):
                    dve.wait_ge(ada_added, d.KD * n + k)
                    dve.scalar_tensor_tensor(out=ada_sum[:], in0=ada_raw[:, k, :], scalar=const["c_act"][:, 0, k:k + 1],
                                             in1=ada_sum[:], op0=ALU.mult, op1=ALU.add).then_inc(ada_added, 1)

            def finish_mod(n):
                dve.wait_ge(mod_summed, n + 1)
                wait(dve, mod_stored, 16 * n)
                dve.tensor_tensor(mod_out[:], ps_m[0:1, 0:MC], mod_bias[:], ALU.add).then_inc(mod_ready, 1)

            def step(s, b):
                t = s - 1
                if in_range(s - 2) and is_latent(s - 2):
                    finish_mod(s - 2 - S0)
                if in_range(s - 2):
                    split_lo(s - 2)
                for n in range(NBLK):
                    if in_range(t) and n in blocks(t):
                        rotate(t, n)
                    if n == 1 and in_range(t) and is_latent(t):
                        add_ada(t - S0)
                    if n == 0 and in_range(s):
                        dve.wait_ge(u_hi_done, s + 1)
                        wait(dve, projected, blocks_before(s - 1))
                        dve.tensor_tensor(u_lo[b][:], ps_x[:], u_hi[b][:].bitcast(F32), ALU.subtract).then_inc(u_lo_done, 1)
                if in_range(t):
                    split_v_lo(t)
            run(dve, step)

        @block.tensor
        def _(pe):
            def turn_x(s, b):
                pe.wait_ge(modulated, s + 1)
                wait(pe, u_lo_done, s)
                for k in range(d.KD):
                    last = pe.transpose(ps_x[:, k, :], x_in[b][:, k * P:(k + 1) * P], const["ident"][:])
                last.then_inc(x_turned, 1)

            def project(t, c, n):
                cols = slice(n * BANK, (n + 1) * BANK)
                pe.wait_ge(u_lo_done, t + 1)
                if n == NBLK - 1:
                    wait(pe, rotated, blocks_before(t))
                    wait(pe, v_lo_done, t)
                elif not isinstance(t, int) or t > S0:
                    pe.wait_ge(rotated, block_count(t - 1, n))
                for k in range(d.KD):
                    for i, (u, w) in enumerate(((u_hi, wqkv_hi), (u_hi, wqkv_lo), (u_lo, wqkv_hi))):
                        last = pe.matmul(ps_q[:, cols], u[c][:, k, :], w[:, k, cols],
                                         start=(k == 0 and i == 0), stop=(k == d.KD - 1 and i == 2))
                last.then_inc(projected, 1)

            def turn_heads(t, n):
                for f, (is_q, h) in fills(t, n):
                    pe.wait_ge(hi_done, t + 1)
                    pe.wait_ge(lo_done, t + 1)
                    bank = ps_t[bank_of(t, f)]
                    wait(pe, moved, fills_before(t) + f + 1 - NB)
                    for i in range(FILL):
                        src = q_split[:, h + i, :, :] if is_q else k_split[:, h + i // 2, i % 2, :, :]
                        last = pe.transpose(bank[:, i, :], src.rearrange("p a n -> p (a n)").bitcast(F32),
                                            const["ident"][:])
                    last.then_inc(turned, 1)

            def sum_ada(n):
                pe.wait_ge(ada_added, d.KD * (n + 1))
                wait(pe, mod_ready, n)
                pe.matmul(ps_m[0:1, 0:MC], const["ones"][:], ada_sum[:], start=True, stop=True).then_inc(mod_summed, 1)

            def step(s, b):
                for n in range(NBLK):
                    if in_range(s - 1) and n in blocks(s - 1):
                        project(s - 1, 1 - b, n)
                    if n == 0 and in_range(s):
                        turn_x(s, b)
                    if in_range(s - 2):
                        turn_heads(s - 2, n)
                if in_range(s - 1) and is_latent(s - 1):
                    sum_ada(s - 1 - S0)
            run(pe, step)



def attention(nc, d, io, scratch, const, k_ctx, v_ctx, aff):
    SLOT = 2 * BANK
    W0, W1, C1 = BANK - d.WIN, BANK, BANK + d.CTX
    KEYS = d.WIN + d.CTX
    KB = KEYS // P
    HG, G, NT = d.HG, d.G, d.NT
    WOC = d.D // G
    LG = BANK // 2
    HP = d.H // 2

    with ExitStack() as ctx:
        sb = lambda n, s, t=F32: ctx.enter_context(nc.sbuf_tensor(n, s, t))
        psum = lambda n, s: ctx.enter_context(nc.psum_tensor(n, s, F32))
        sem = lambda n: ctx.enter_context(nc.semaphore(n))
        wo_raw = sb("wo_raw", [P, HP, WOC])
        wo_hi = sb("wo_hi", [P, HP, d.D], F32R)
        wo_lo = sb("wo_lo", [P, HP, d.D], F32R)
        q_in = [sb(f"q_in{b}", [P, HG, P], F32R) for b in range(2)]
        k_in = [sb(f"k_in{b}", [P, 2, d.WIN], F32R) for b in range(2)]
        v_in = [sb(f"v_in{b}", [P, 3, 2 * d.DH], F32R) for b in range(2)]
        x_in = sb("xa_in", [P, d.D])
        prob = [sb(f"prob{g}", [P, HG, KEYS + 1]) for g in range(G)]
        pt_hi = [sb(f"pt_hi{b}", [P, HG, P], F32R) for b in range(2)]
        pt_lo = [sb(f"pt_lo{b}", [P, HG, P], F32R) for b in range(2)]
        o_low = sb("o_low", [d.DH, HG, P])
        o_sum = sb("o_sum", [P, HP, P])
        o_hi = sb("o_hi", [P, HP, P], F32R)
        o_lo = sb("o_lo", [P, HP, P], F32R)
        z = sb("z", [P, d.D])
        t_out = sb("t_out", [P, d.D])
        r_out = sb("r_out", [P, d.D])
        tt = sb("tt", [P, d.KD, P])
        row_g1 = sb("row_g1", [P, d.D])
        row_tg = sb("row_tg", [P, d.D])
        row_tb = sb("row_tb", [P, d.D])
        row_rg = sb("row_rg", [P, d.D])
        row_rb = sb("row_rb", [P, d.D])
        router = sb("router", [P, d.KD, d.E])
        mask = sb("mask", [P, 3, P], BF16)
        sink = sb("sink", [P, d.H])
        sink_part = [sb(f"sink_part{n}", [P, d.H], BF16) for n in range(3)]
        sink_key = sb("sink_key", [P, d.H], BF16)
        ones = sb("ones3", [P, P], BF16)
        neg_max = [sb(f"neg_max{b}", [P, HG]) for b in range(2)]
        total = [sb(f"total{g}", [P, HG]) for g in range(G)]
        inv = [sb(f"inv{g}", [P, HG]) for g in range(G)]
        stats = sb("stats", [P, 2, 6])
        mean_var = sb("mean_var", [P, 2])
        var_eps = sb("var_eps", [P, 1])
        minus_half = sb("minus_half", [P, 1])
        rstd = sb("rstd", [P, 1])
        lg_t = sb("lg_t", [d.E, P])
        lg_max = sb("lg_max", [P, 1])
        lg_exp = sb("lg_exp", [P, d.E])
        lg_sum = sb("lg_sum", [P, 1])
        lg_inv = sb("lg_inv", [P, 1])
        ps_s = [psum(f"ps_s{b}", [P, SLOT]) for b in range(2)]
        ps_t = [psum(f"ps_pt{b}", [P, HG, P]) for b in range(2)]
        ps_o = psum("ps_o", [P, HG, P])
        ps_y = psum("ps_y", [P, BANK])

        rows_loaded, rows_mid, rows_ready = sem("rows_loaded"), sem("rows_mid"), sem("rows_ready")
        sink_loaded = sem("sink_loaded")
        masks_made, sink_ready, half_made = sem("masks_made"), sem("sink_ready"), sem("half_made")
        router_loaded = sem("router_loaded")
        wo_loaded, wo_hi_done, wo_lo_done = sem("wo_loaded"), sem("wo_hi_done"), sem("wo_lo_done")
        qk_loaded = [sem(f"qk_loaded{b}") for b in range(2)]
        v_loaded = [sem(f"v_loaded{b}") for b in range(2)]
        x_loaded = sem("xa_loaded")
        scored, maxed, expd = sem("scored"), sem("maxed"), sem("expd")
        inverted, normed = sem("inverted"), sem("normed")
        turned, pt_hi_done, pt_lo_done, pv_done = sem("p_turned"), sem("pt_hi_done"), sem("pt_lo_done"), sem("pv_done")
        o_copied, o_added, o_hi_done, o_lo_done = sem("o_copied"), sem("o_added"), sem("o_hi_done"), sem("o_lo_done")
        y_summed, y_gated, z_done, stats_done = sem("y_summed"), sem("y_gated"), sem("z_done"), sem("stats_done")
        mv_done, var_done, rstd_done, n_done = sem("mv_done"), sem("var_done"), sem("rstd_done"), sem("n_done")
        scaled, t_done, r_done = sem("scaled3"), sem("t_done"), sem("r_done")
        t_stored, r_stored, aff_stored = sem("t_stored"), sem("r_stored"), sem("aff_stored")
        tt_turned, tt_moved, lg_summed, lg_moved, lg_turned = (sem("tt_turned"), sem("tt_moved"), sem("lg_summed"),
                                                               sem("lg_moved"), sem("lg_turned"))
        lg_maxed, lg_expd, lg_inverted, aff_done = sem("lg_maxed"), sem("lg_expd"), sem("lg_inverted"), sem("aff_done")
        block = ctx.enter_context(nc.Block())

        def run(eng, body, ahead=0):
            for i in range(3):
                body(i)
            with eng.Fori(3, NT - 1) as i:
                body(i)
            for i in range(NT - 1, NT + 3):
                body(i)

        def tile(i):
            return not isinstance(i, int) or 0 <= i < NT

        ORDER = (("S", 0), ("T", 0), ("S", 1), ("T", 1), ("P", 0), ("L", 0), ("T", 2), ("P", 1), ("S", 2), ("L", 1),
                 ("T", 3), ("P", 2), ("L", 2), ("T", 4), ("P", 3), ("S", 3), ("L", 3), ("P", 4), ("L", 4))

        ORDER_ACT = (("T", 0), ("S", 0), ("T", 1), ("T", 2), ("S", 1), ("T", 3), ("S", 2), ("T", 4), ("S", 3))

        UNITS = {place: k for k, place in enumerate((("T", 2), ("P", 1), ("S", 2), ("L", 1),
                                                     ("L", 2), ("P", 3), ("L", 3), ("L", 4)))}

        def shift(i, g, steps):
            return i + (g + steps) // G, (g + steps) % G

        @block.sync
        def _(sp):
            sp.dma_start(sink[:], io["attn_sink"].broadcast_to([P, d.H])).then_inc(sink_loaded, 16)

            def load_qk(i, g):
                qt = scratch["qt"][bass.ds(i, 1), :, g * HG:(g + 1) * HG, :].rearrange("t p h n -> p (t h) n")
                sp.dma_start(q_in[g % 2][:].bitcast(F32), qt).then_inc(qk_loaded[g % 2], 16)
                sp.dma_start(k_in[g % 2][:].bitcast(F32),
                             scratch["kt"][:, g, :, bass.ds(i * P, d.WIN)]).then_inc(qk_loaded[g % 2], 16)

            def load_v(i, g):
                sp.dma_start(v_in[g % 2][:].bitcast(F32), scratch["v"][bass.ds(i, 3), :, g, :]
                             .rearrange("t p n -> p t n")).then_inc(v_loaded[g % 2], 16)

            for g in range(2):
                load_qk(0, g)
                load_v(0, g)

            mod = scratch["mod"]
            for row, src in ((row_g1, mod[0:1, 2 * d.D:3 * d.D]), (row_tg, io["ln1_g"]), (row_tb, io["ln1_b"]),
                             (row_rg, mod[0:1, 4 * d.D:5 * d.D]), (row_rb, mod[0:1, 3 * d.D:4 * d.D])):
                sp.dma_start(row[:], src.broadcast_to([P, d.D])).then_inc(rows_loaded, 16)
            sp.dma_start(router[:], io["moe_router"][0].rearrange("(k p) e -> p k e", p=P)).then_inc(router_loaded, 16)

            def body(i):
                for g in range(G):
                    ni, ng = shift(i, g, 2)
                    if tile(i) and tile(ni):
                        sp.wait_ge(scored, 16 * i + HG * (g + 1))
                        load_qk(ni, ng)
                    pi, pg = shift(i, g, -2)
                    if tile(pi) and tile(i):
                        sp.wait_ge(pv_done, KB * (4 * pi + pg + 1))
                        load_v(i, g)
                    if g == 2 and tile(i - 1):
                        wait(sp, z_done, 2 * (i - 1))
                        sp.dma_start(x_in[:], io["x"][0, bass.ds((i - 1) * P, P), :]).then_inc(x_loaded, 16)
                    if g == 3 and tile(i - 2):
                        sp.wait_ge(t_done, i - 1)
                        sp.dma_start(scratch["tok"][bass.ds((i - 2) * P, P), 0:d.D], t_out[:]).then_inc(t_stored, 16)
                    if g == 0 and tile(i - 3):
                        sp.wait_ge(r_done, i - 2)
                        sp.dma_start(scratch["res"][bass.ds((i - 3) * P, P), :], r_out[:]).then_inc(r_stored, 16)
                    if g == 3 and tile(i - 3):
                        sp.wait_ge(aff_done, i - 2)
                        sp.dma_start(scratch["tok"][bass.ds((i - 3) * P, P), d.D:d.D + d.E],
                                     aff[:, bass.ds(i - 3, 1), :].rearrange("p t e -> p (t e)")).then_inc(aff_stored, 16)
            run(sp, body)
            for s in (t_stored, r_stored, aff_stored):
                sp.wait_ge(s, 16 * NT)

        @block.gpsimd
        def _(pool):
            pool.memset(minus_half[:], -0.5).then_inc(half_made, 1)
            pool.memset(mask[:, 0:2, :], 0.0).then_inc(masks_made, 1)
            pool.memset(mask[:, 2, :], NEG).then_inc(masks_made, 1)
            pool.memset(ones[:], 1.0).then_inc(masks_made, 1)
            pool.wait_ge(masks_made, 1)
            pool.affine_select(out=mask[:, 0, :], in_=mask[:, 0, :], compare_op=ALU.is_ge, fill=NEG, base=0,
                               pattern=[[1, P]], channel_multiplier=-1).then_inc(masks_made, 1)
            pool.affine_select(out=mask[:, 1, :], in_=mask[:, 1, :], compare_op=ALU.is_ge, fill=NEG, base=0,
                               pattern=[[-1, P]], channel_multiplier=1).then_inc(masks_made, 1)

            def body(i):
                for g in range(G):
                    t = i - 2
                    if g == 2 and tile(t):
                        pool.wait_ge(var_done, t + 1)
                        pool.wait_ge(half_made, 1)
                        pool.tensor_tensor(rstd[:], var_eps[:], minus_half[:], ALU.pow).then_inc(rstd_done, 1)
                        pool.wait_ge(rstd_done, t + 1)
                        apart(pool, const["carried"])
                        pool.tensor_scalar(z[:], z[:], mean_var[:, 0:1], rstd[:], ALU.subtract, ALU.mult).then_inc(n_done, 1)
                    pi, pg = shift(i, g, -1)
                    if tile(pi):
                        pool.wait_ge(inverted, 4 * pi + pg + 1)
                        apart(pool, const["carried"])
                        for h in range(HG):
                            last = pool.tensor_scalar(prob[pg][:, h, :], prob[pg][:, h, :],
                                                      inv[pg][:, h:h + 1], 1.0, ALU.mult, ALU.mult)
                        last.then_inc(normed, 1)
                    if g == 2 and tile(i - 1):
                        pool.wait_ge(o_hi_done, i)
                        wait(pool, y_summed, 2 * (i - 1))
                        pool.tensor_tensor(o_lo[:], o_sum[:], o_hi[:].bitcast(F32), ALU.subtract).then_inc(o_lo_done, 1)
                    if g == 2 and tile(t):
                        pool.wait_ge(rows_ready, 1)
                        pool.wait_ge(n_done, t + 1)
                        wait(pool, t_stored, 16 * t)
                        wait(pool, tt_turned, 2 * t)
                        pool.tensor_tensor(t_out[:], z[:], row_tg[:], ALU.mult).then_inc(scaled, 1)
                        pool.wait_ge(scaled, 2 * t + 1)
                        pool.tensor_tensor(t_out[:], t_out[:], row_tb[:], ALU.add).then_inc(t_done, 1)
                    if g == 3 and tile(t):
                        wait(pool, r_stored, 16 * t)
                        pool.tensor_tensor(r_out[:], z[:], row_rg[:], ALU.mult).then_inc(scaled, 1)
                        pool.wait_ge(scaled, 2 * t + 2)
                        pool.tensor_tensor(r_out[:], r_out[:], row_rb[:], ALU.add).then_inc(r_done, 1)
            run(pool, body)

        @block.scalar
        def _(act):
            def load_wo(n):
                wait(act, wo_hi_done, n)
                wait(act, wo_lo_done, n)
                act.dma_start(wo_raw[:], io["attn_w_o"][0].rearrange("(k p) n -> p k n", p=P)
                              [:, :, n * WOC:(n + 1) * WOC]).then_inc(wo_loaded, 16)

            def split_wo(n):
                act.wait_ge(wo_loaded, 16 * (n + 1))
                act.activation(wo_hi[:, :, n * WOC:(n + 1) * WOC], wo_raw[:], ACT.Copy).then_inc(wo_hi_done, 1)

            def exp(i, g, h):
                n = 16 * i + HG * g + h
                if h == 0:
                    wait(act, turned, KB * (4 * (i - 1) + g + 1))
                act.wait_ge(maxed, n + 1)
                act.activation(prob[g][:, h, :], ps_s[h % 2][:, W0:C1 + 1], ACT.Exp,
                               bias=neg_max[g % 2][:, h:h + 1], accum_out=total[g][:, h:h + 1]).then_inc(expd, 1)

            def part(i, g, j):
                m = KB * (4 * i + g) + j
                b = (KB * g + j) % 2
                act.wait_ge(turned, m + 1)
                wait(act, pv_done, m - 1)
                act.activation(pt_hi[b][:], ps_t[b][:], ACT.Copy).then_inc(pt_hi_done, 1)

            def move_tt(t, half):
                act.wait_ge(tt_turned, 2 * t + half + 1)
                if half == 0:
                    wait(act, lg_summed, t)
                act.activation(tt[:, 4 * half:4 * half + 4, :], ps_y[:].rearrange("p (k n) -> p k n", n=P),
                               ACT.Copy).then_inc(tt_moved, 1)

            def body(i):
                for g in range(G):
                    if isinstance(i, int) and i == 0:
                        load_wo(g)
                    pi, pg = shift(i, g, -2)
                    t = i - 3
                    li, lg = shift(i, g, -3)
                    if tile(li):
                        m = 4 * li + lg
                        act.wait_ge(pv_done, KB * (m + 1))
                        wait(act, o_added, m)
                        act.activation(o_low[:], ps_o[d.DH:P], ACT.Copy).then_inc(o_copied, 1)
                    for what, n in ORDER_ACT:
                        if tile(t) and g == 1 and (what, n) in (("S", 2), ("S", 3)):
                            move_tt(t, n - 2)
                        if tile(t) and g == 2 and (what, n) == ("T", 1):
                            act.wait_ge(lg_summed, t + 1)
                            act.activation(lg_t[:], ps_y[0:d.E, 0:P], ACT.Copy).then_inc(lg_moved, 1)
                        if what == "S" and tile(i):
                            exp(i, g, n)
                        if what == "T" and tile(pi):
                            part(pi, pg, n)
                        if (what, n) == ("T", 1) and g == 2 and tile(i - 1):
                            act.wait_ge(o_added, 4 * i)
                            wait(act, y_summed, 2 * (i - 1))
                            act.activation(o_hi[:], o_sum[:], ACT.Copy).then_inc(o_hi_done, 1)
                    if g == 2 and tile(t):
                        act.wait_ge(lg_maxed, t + 1)
                        act.activation(lg_exp[:], ps_y[:, LG:LG + d.E], ACT.Exp, bias=lg_max[:],
                                       accum_out=lg_sum[:]).then_inc(lg_expd, 1)
                    if isinstance(i, int) and i == 0:
                        split_wo(g)
            run(act, body)

        @block.vector
        def _(dve):
            dve.wait_ge(sink_loaded, 16)
            dve.memset(sink_key[:], 0.0).then_inc(sink_ready, 1)
            for n in range(3):
                dve.tensor_copy(sink_part[n][:], sink[:]).then_inc(sink_ready, 1)
                dve.wait_ge(sink_ready, 3 * n + 2 if n else 2)
                dve.tensor_copy(sink_key[32 * n:32 * n + 1, :], sink_part[n][32 * n:32 * n + 1, :]).then_inc(sink_ready, 1)
                if n < 2:
                    dve.tensor_tensor(sink[:], sink[:], sink_part[n][:], ALU.subtract).then_inc(sink_ready, 1)
                    dve.wait_ge(sink_ready, 3 * n + 4)

            def prepare_rows():
                dve.wait_ge(rows_loaded, 80)
                dve.tensor_scalar(row_rg[:], row_rg[:], 1.0, None, ALU.add).then_inc(rows_mid, 1)
                dve.tensor_scalar(z[:], row_tg[:], d.alpha, None, ALU.mult).then_inc(rows_mid, 1)
                dve.tensor_scalar(t_out[:], row_tb[:], d.alpha, None, ALU.mult).then_inc(rows_mid, 1)
                dve.wait_ge(rows_mid, 3)
                dve.tensor_tensor(row_tg[:], row_tg[:], row_rg[:], ALU.mult).then_inc(rows_mid, 1)
                dve.tensor_tensor(row_tb[:], row_tb[:], row_rg[:], ALU.mult).then_inc(rows_mid, 1)
                dve.wait_ge(rows_mid, 5)
                dve.tensor_tensor(row_tb[:], row_tb[:], row_rb[:], ALU.add).then_inc(rows_mid, 1)
                dve.wait_ge(rows_mid, 6)
                dve.tensor_copy(row_rg[:], z[:]).then_inc(rows_mid, 1)
                dve.tensor_copy(row_rb[:], t_out[:]).then_inc(rows_mid, 1)
                dve.wait_ge(rows_mid, 8)
                dve.sem_inc(rows_ready, 1)

            def split_wo(n):
                cols = slice(n * WOC, (n + 1) * WOC)
                dve.wait_ge(wo_hi_done, n + 1)
                dve.tensor_tensor(wo_lo[:, :, cols], wo_raw[:], wo_hi[:, :, cols].bitcast(F32),
                                  ALU.subtract).then_inc(wo_lo_done, 1)

            def score_max(i, g, h):
                n = 16 * i + HG * g + h
                dve.wait_ge(scored, n + 1)
                if h == 0:
                    wait(dve, expd, HG * (4 * i + g - 1))
                dve.tensor_reduce(neg_max[g % 2][:, h:h + 1], ps_s[h % 2][:, W0:C1 + 1], AX_X, ALU.max,
                                  negate=True).then_inc(maxed, 1)

            def invert(i, g):
                m = 4 * i + g
                dve.wait_ge(expd, HG * (m + 1))
                wait(dve, normed, m - 3)
                dve.reciprocal(inv[g][:], total[g][:]).then_inc(inverted, 1)

            def part(i, g, j):
                m = KB * (4 * i + g) + j
                b = (KB * g + j) % 2
                dve.wait_ge(pt_hi_done, m + 1)
                wait(dve, pv_done, m - 1)
                dve.tensor_tensor(pt_lo[b][:], ps_t[b][:], pt_hi[b][:].bitcast(F32), ALU.subtract).then_inc(pt_lo_done, 1)

            def join(i, g):
                m = 4 * i + g
                dve.wait_ge(o_copied, m + 1)
                if g == 0:
                    wait(dve, o_lo_done, i)
                for odd in range(2):
                    last = dve.tensor_tensor(o_sum[odd * d.DH:(odd + 1) * d.DH, 2 * g:2 * g + 2, :],
                                             ps_o[0:d.DH, odd:HG:2, :], o_low[:, odd:HG:2, :], ALU.add)
                last.then_inc(o_added, 1)

            def affinities(t):
                dve.wait_ge(lg_expd, t + 1)
                dve.reciprocal(lg_inv[:], lg_sum[:]).then_inc(lg_inverted, 1)
                dve.wait_ge(lg_inverted, t + 1)
                dve.tensor_scalar(aff[:, bass.ds(t, 1), :].rearrange("p t e -> p (t e)"), lg_exp[:], lg_inv[:],
                                  None, ALU.mult).then_inc(aff_done, 1)

            def gate_in(t, half):
                n = 2 * t + half
                cols = slice(half * BANK, (half + 1) * BANK)
                dve.wait_ge(y_summed, n + 1)
                if half == 0:
                    wait(dve, r_done, t)
                dve.tensor_tensor(z[:, cols], ps_y[:], row_g1[:, cols], ALU.mult).then_inc(y_gated, 1)

            def add_in(t, half):
                n = 2 * t + half
                cols = slice(half * BANK, (half + 1) * BANK)
                dve.wait_ge(y_gated, n + 1)
                dve.wait_ge(x_loaded, 16 * (t + 1))
                dve.scalar_tensor_tensor(out=z[:, cols], in0=x_in[:, cols], scalar=d.alpha, in1=z[:, cols],
                                         op0=ALU.mult, op1=ALU.add).then_inc(z_done, 1)
                dve.wait_ge(z_done, n + 1)
                dve.bn_stats(stats[:, half, :], z[:, cols]).then_inc(stats_done, 1)
                if half == 1:
                    dve.wait_ge(stats_done, n + 1)
                    apart(dve, const["carried"])
                    dve.bn_aggr(mean_var[:], stats[:].rearrange("p a b -> p (a b)")).then_inc(mv_done, 1)
                    dve.wait_ge(mv_done, t + 1)
                    dve.tensor_scalar(var_eps[:], mean_var[:, 1:2], d.eps, None, ALU.add).then_inc(var_done, 1)

            def body(i):
                for g in range(G):
                    pi, pg = shift(i, g, -2)
                    for what, n in ORDER:
                        if what == "S" and tile(i):
                            score_max(i, g, n)
                        if (what, n) == ("S", 0):
                            li, lg = shift(i, g, -1)
                            if tile(li):
                                invert(li, lg)
                            li, lg = shift(i, g, -3)
                            if tile(li):
                                join(li, lg)
                        if what == "T" and tile(pi):
                            part(pi, pg, n)
                        if (what, n) == ("T", 0) and g in (0, 1) and tile(i - 2):
                            gate_in(i - 2, g)
                        if (what, n) == ("T", 2) and g in (0, 1) and tile(i - 2):
                            add_in(i - 2, g)
                        if (what, n) == ("T", 4) and g == 3 and tile(i - 3):
                            affinities(i - 3)
                    if g == 2 and tile(i - 3):
                        dve.wait_ge(lg_turned, i - 2)
                        dve.tensor_reduce(lg_max[:], ps_y[:, LG:LG + d.E], AX_X, ALU.max, negate=True).then_inc(lg_maxed, 1)
                    if isinstance(i, int) and i == 0:
                        split_wo(g)
                        if g == G - 1:
                            prepare_rows()
            run(dve, body)

        @block.tensor
        def _(pe):
            pe.wait_ge(masks_made, 5)
            pe.wait_ge(sink_ready, 9)

            def scores(i, g, h):
                n = 16 * i + HG * g + h
                s, q, k = ps_s[h % 2], q_in[g % 2], k_in[g % 2]
                if h == 0:
                    pe.wait_ge(qk_loaded[g % 2], 32 * (2 * i + g // 2 + 1))
                wait(pe, expd, n - 1)
                for part in range(2):
                    pe.matmul(s[:, W0:W1], q[:, h, :], k[:, part, :], start=(part == 0), stop=False)
                left = 2 if isinstance(i, int) and i == 0 else 0
                right = 2 if isinstance(i, int) and i == NT - 1 else 1
                pe.matmul(s[:, W0:W0 + P], const["ident_bf"][:], mask[:, left, :], start=False, stop=False)
                pe.matmul(s[:, W1 - P:W1], const["ident_bf"][:], mask[:, right, :], start=False, stop=True)
                for part in range(2):
                    pe.matmul(s[:, W1:C1], q[:, h, :], k_ctx[:, g, part, :], start=(part == 0), stop=(part == 1))
                column = HG * g + h
                last = pe.matmul(s[:, C1:C1 + 1], ones[:], sink_key[:, column:column + 1], start=True, stop=True)
                last.then_inc(scored, 1)

            def turn(i, g, j):
                m = KB * (4 * i + g) + j
                b = (KB * g + j) % 2
                if j == 0:
                    pe.wait_ge(normed, 4 * i + g + 1)
                wait(pe, pt_lo_done, m - 1)
                for h in range(HG):
                    last = pe.transpose(ps_t[b][:, h, :], prob[g][:, h, j * P:(j + 1) * P], const["ident"][:])
                last.then_inc(turned, 1)

            def product(i, g, j, part):
                m = KB * (4 * i + g) + j
                b = (KB * g + j) % 2
                v = v_in[g % 2][:, j, :] if j < 3 else v_ctx[:, j - 3, g, :]
                if part == "P":
                    if j == 0:
                        pe.wait_ge(v_loaded[g % 2], 16 * (2 * i + g // 2 + 1))
                        wait(pe, o_added, 4 * i + g)
                    pe.wait_ge(pt_hi_done, m + 1)
                    pe.matmul(ps_o[:], v, pt_hi[b][:], start=(j == 0), stop=False)
                else:
                    pe.wait_ge(pt_lo_done, m + 1)
                    pe.matmul(ps_o[:], v, pt_lo[b][:], start=False, stop=(j == KB - 1)).then_inc(pv_done, 1)

            def output(t, half, k):
                cols = slice(half * BANK, (half + 1) * BANK)
                if k == 0:
                    if half == 0:
                        pe.wait_ge(o_lo_done, t + 1)
                        pe.wait_ge(wo_lo_done, G)
                        wait(pe, lg_expd, t - 1)
                    wait(pe, y_gated, 2 * t + half)
                for n, (o, w) in enumerate(((o_hi, wo_hi), (o_hi, wo_lo), (o_lo, wo_hi))):
                    last = pe.matmul(ps_y[:], o[:, k, :], w[:, k, cols], start=(k == 0 and n == 0),
                                     stop=(k == HP - 1 and n == 2))
                if k == HP - 1:
                    last.then_inc(y_summed, 1)

            def turn_tokens(t, half):
                if half == 0:
                    pe.wait_ge(t_done, t + 1)
                    wait(pe, lg_expd, t)
                    pe.wait_ge(y_gated, min(2 * t + 4, 2 * NT) if isinstance(t, int) else 2 * t + 4)
                wait(pe, tt_moved, 2 * t + half)
                for k in range(4):
                    cols = slice((4 * half + k) * P, (4 * half + k + 1) * P)
                    last = pe.transpose(ps_y[:, k * P:(k + 1) * P], t_out[:, cols], const["ident"][:])
                last.then_inc(tt_turned, 1)

            def logits(t):
                pe.wait_ge(tt_moved, 2 * t + 2)
                pe.wait_ge(router_loaded, 16)
                for k in range(d.KD):
                    last = pe.matmul(ps_y[0:d.E, 0:P], router[:, k, :], tt[:, k, :], start=(k == 0), stop=(k == d.KD - 1))
                last.then_inc(lg_summed, 1)

            def turn_logits(t):
                pe.wait_ge(lg_moved, t + 1)
                apart(pe, const["carried"])
                pe.transpose(ps_y[:, LG:LG + d.E], lg_t[:], const["ident"][0:d.E, 0:d.E]).then_inc(lg_turned, 1)

            def body(i):
                for g in range(G):
                    pi, pg = shift(i, g, -2)
                    t = i - 3
                    for what, n in ORDER:
                        if tile(t) and g == 1 and (what, n) in (("S", 2), ("S", 3)):
                            turn_tokens(t, n - 2)
                        if tile(t) and g == 2 and (what, n) == ("T", 1):
                            logits(t)
                        if tile(t) and g == 2 and (what, n) == ("S", 2):
                            turn_logits(t)
                        if (what, n) in UNITS:
                            if g == 3 and tile(i - 1):
                                output(i - 1, 0, UNITS[what, n])
                            if g == 0 and tile(i - 2):
                                output(i - 2, 1, UNITS[what, n])
                        if what == "S" and tile(i):
                            scores(i, g, n)
                        if what == "T" and tile(pi):
                            turn(pi, pg, n)
                        if what in "PL" and tile(pi):
                            product(pi, pg, n, what)
            run(pe, body)



class ExpertWeights:

    KH = 4
    RAW, RING = 3, 3

    def __init__(self, nc, d, io, ctx):
        sb = lambda n, s, t=F32: ctx.enter_context(nc.sbuf_tensor(n, s, t))
        sem = lambda n: ctx.enter_context(nc.semaphore(n))
        self.FC = d.F // BANK
        self.HF = d.F // P
        self.PIECES = 2 * self.FC + 2 * (self.HF // (2 * self.KH))
        self.SUBS = 2 * self.PIECES
        view = lambda name: io[name][0].rearrange("e (k p) n -> e p k n", p=P)
        w1, w3, w2 = view("moe_w1"), view("moe_w3"), view("moe_w2")
        self.pieces = [(w, 0, c) for c in range(self.FC) for w in (w1, w3)]
        self.pieces += [(w2, k, c) for c in range(2) for k in range(0, self.HF, 2 * self.KH)]
        self.raw = [sb(f"raw{b}", [P, 2 * self.KH, BANK]) for b in range(self.RAW)]
        self.w_hi = [sb(f"w_hi{b}", [P, self.KH, BANK], F32R) for b in range(self.RING)]
        self.w_lo = [sb(f"w_lo{b}", [P, self.KH, BANK], F32R) for b in range(self.RING)]
        self.raw_loaded = [sem(f"raw_loaded{b}") for b in range(self.RAW)]
        self.w_hi_done, self.w_lo_done, self.used = sem("ew_hi_done"), sem("ew_lo_done"), sem("used")

    def load(self, sp, e, n):
        w, k, c = self.pieces[n]
        b = n % self.RAW
        wait(sp, self.w_lo_done, self.SUBS * e + 2 * (n - self.RAW) + 2)
        sp.dma_start(self.raw[b][:], w[bass.ds(e, 1), :, k:k + 2 * self.KH, c * BANK:(c + 1) * BANK]
                     .rearrange("e p k n -> (e p) k n")).then_inc(self.raw_loaded[b], 16)

    def convert(self, eng, e, u, kind):
        n = self.SUBS * e + u
        b, r = u % self.RING, (u // 2) % self.RAW
        src = self.raw[r][:, (u % 2) * self.KH:(u % 2 + 1) * self.KH, :]
        wait(eng, self.used, n - self.RING + 1)
        if kind == "hi":
            eng.wait_ge(self.raw_loaded[r], 16 * ((self.PIECES // self.RAW) * e + (u // 2) // self.RAW + 1))
            eng.activation(self.w_hi[b][:], src, ACT.Copy).then_inc(self.w_hi_done, 1)
        else:
            eng.wait_ge(self.w_hi_done, n + 1)
            eng.tensor_tensor(self.w_lo[b][:], src, self.w_hi[b][:].bitcast(F32), ALU.subtract).then_inc(self.w_lo_done, 1)



def choice(nc, d, const, stream, aff, slot_of):
    NB = 30
    NE = d.NT * d.E
    with ExitStack() as ctx:
        sb = lambda n, s, t=F32: ctx.enter_context(nc.sbuf_tensor(n, s, t))
        psum = lambda n, s: ctx.enter_context(nc.psum_tensor(n, s, F32))
        sem = lambda n: ctx.enter_context(nc.semaphore(n))
        ones = sb("ones_bf", [P, P], BF16)
        upto = sb("upto_bf", [P, P], BF16)
        bit = sb("bit", [P, 1], I32)
        best = sb("best", [P, d.E])
        cand = sb("cand", [P, d.E])
        kept = sb("kept", [P, d.E])
        reach = sb("reach", [P, d.NT, d.E], BF16)
        count = sb("count", [P, d.E], BF16)
        above = sb("above", [P, d.NT, d.E], BF16)
        equal = sb("equal", [P, d.NT, d.E], BF16)
        missing = sb("missing", [P, d.E])
        early = sb("early", [P, d.NT, d.E])
        chosen = sb("chosen", [P, d.NT, d.E], BF16)
        ps_n = psum("ps_n", [P, BANK])
        ps_r = psum("ps_r", [P, BANK])
        made, started = sem("made4"), sem("started")
        tried, compared, counted, summed, judged, raised, halved = (sem("tried"), sem("compared"), sem("counted"),
                                                                    sem("summed4"), sem("judged"), sem("raised"), sem("halved"))
        masks_done, count_done, above_summed, missing_done = sem("masks_done"), sem("count_done"), sem("above_summed"), sem("missing_done")
        ranked, early_done, chosen_done, placed, slots_mid, slots_done = (sem("ranked"), sem("early_done"), sem("chosen_done"),
                                                                          sem("placed"), sem("slots_mid"), sem("slots_done"))
        block = ctx.enter_context(nc.Block())

        def over_tiles(ap):
            return copies(ap, 1, d.NT)

        @block.sync
        def _(sp):
            for n in range(stream.RAW):
                stream.load(sp, 0, n)

        @block.scalar
        def _(act):
            for u in range(stream.RING):
                stream.convert(act, 0, u, "hi")

        @block.gpsimd
        def _(pool):
            pool.memset(ones[:], 1.0).then_inc(made, 1)
            pool.memset(upto[:], 1.0).then_inc(made, 1)
            pool.wait_ge(made, 2)
            pool.affine_select(out=upto[:], in_=upto[:], compare_op=ALU.is_ge, fill=0.0, base=0,
                               pattern=[[1, P]], channel_multiplier=-1).then_inc(made, 1)
            for u in range(stream.RING):
                stream.convert(pool, 0, u, "lo")

        @block.vector
        def _(dve):
            dve.memset(bit[:], 1 << (NB - 1)).then_inc(started, 1)
            dve.memset(best[:], 0.0).then_inc(started, 1)
            dve.wait_ge(started, 2)

            def try_bit(i):
                wait(dve, raised, i)
                wait(dve, halved, i)
                dve.tensor_tensor(cand[:].bitcast(I32), best[:].bitcast(I32), bit[:].broadcast_to([P, d.E]),
                                  ALU.bitwise_or).then_inc(tried, 1)
                dve.wait_ge(tried, i + 1)
                dve.tensor_tensor(reach[:], aff[:], over_tiles(cand[:]), ALU.is_ge).then_inc(compared, 1)
                dve.wait_ge(compared, i + 1)
                with nc.allow_low_precision(reason="counts up to 16 are exact"):
                    dve.tensor_reduce(count[:], reach[:].rearrange("p t e -> p e t"), AX_X, ALU.add).then_inc(counted, 1)
                dve.tensor_scalar(bit[:], bit[:], 1, None, ALU.logical_shift_right).then_inc(halved, 1)
                dve.wait_ge(summed, i + 1)
                dve.scalar_tensor_tensor(out=kept[:], in0=ps_n[:, 0:d.E], scalar=float(d.CAP), in1=cand[:],
                                         op0=ALU.is_ge, op1=ALU.mult).then_inc(judged, 1)
                dve.wait_ge(judged, i + 1)
                dve.tensor_tensor(best[:], best[:], kept[:], ALU.max).then_inc(raised, 1)
            peeled(dve, NB, try_bit)
            dve.wait_ge(raised, NB)
            dve.tensor_tensor(above[:], aff[:], over_tiles(best[:]), ALU.is_gt).then_inc(masks_done, 1)
            dve.tensor_tensor(equal[:], aff[:], over_tiles(best[:]), ALU.is_equal).then_inc(masks_done, 1)
            dve.wait_ge(masks_done, 1)
            with nc.allow_low_precision(reason="counts up to 16 are exact"):
                dve.tensor_reduce(count[:], above[:].rearrange("p t e -> p e t"), AX_X, ALU.add).then_inc(count_done, 1)
            dve.wait_ge(above_summed, 1)
            dve.tensor_scalar(missing[:], ps_n[:, 0:d.E], -1.0, float(d.CAP), ALU.mult, ALU.add).then_inc(missing_done, 1)
            dve.wait_ge(missing_done, 1)
            dve.wait_ge(ranked, 1)
            dve.tensor_tensor(early[:], ps_r[:, 0:NE].rearrange("p (t e) -> p t e", e=d.E), over_tiles(missing[:]),
                              ALU.is_le).then_inc(early_done, 1)
            dve.wait_ge(early_done, 1)
            dve.tensor_tensor(early[:], early[:], equal[:], ALU.mult).then_inc(early_done, 1)
            dve.wait_ge(early_done, 2)
            dve.tensor_tensor(chosen[:], early[:], above[:], ALU.add).then_inc(chosen_done, 1)
            dve.wait_ge(placed, 1)
            dve.tensor_tensor(slot_of[:], ps_r[:, 0:NE].rearrange("p (t e) -> p t e", e=d.E), chosen[:],
                              ALU.mult).then_inc(slots_mid, 1)
            dve.wait_ge(slots_mid, 1)
            dve.tensor_scalar(slot_of[:], slot_of[:], -1.0, None, ALU.add).then_inc(slots_done, 1)

        @block.tensor
        def _(pe):
            def rank(of):
                flat = of[:].rearrange("p t e -> p (t e)")
                for back in range(d.NT):
                    last = pe.matmul(ps_r[:, back * d.E:NE], (ones if back else upto)[:], flat[:, 0:NE - back * d.E],
                                     start=(back == 0), stop=(back == d.NT - 1))
                return last

            pe.wait_ge(made, 3)

            def count_all(i):
                pe.wait_ge(counted, i + 1)
                wait(pe, judged, i)
                pe.matmul(ps_n[:, 0:d.E], ones[:], count[:], start=True, stop=True).then_inc(summed, 1)
            peeled(pe, NB, count_all)
            pe.wait_ge(masks_done, 2)
            rank(equal).then_inc(ranked, 1)
            pe.wait_ge(count_done, 1)
            pe.wait_ge(judged, NB)
            pe.matmul(ps_n[:, 0:d.E], ones[:], count[:], start=True, stop=True).then_inc(above_summed, 1)
            pe.wait_ge(chosen_done, 1)
            rank(chosen).then_inc(placed, 1)



def experts(nc, d, io, scratch, const, stream, slot_of):
    KH, RING, FC, HF, SUBS = stream.KH, stream.RING, stream.FC, stream.HF, stream.SUBS
    w_hi, w_lo, w_hi_done, w_lo_done, used = stream.w_hi, stream.w_lo, stream.w_hi_done, stream.w_lo_done, stream.used
    convert = stream.convert
    NS = d.CAP // P
    FILLS = 2 * FC + d.KD // 2
    TB = 3
    LAST = d.E - 1

    with ExitStack() as ctx:
        sb = lambda n, s, t=F32: ctx.enter_context(nc.sbuf_tensor(n, s, t))
        psum = lambda n, s: ctx.enter_context(nc.psum_tensor(n, s, F32))
        sem = lambda n: ctx.enter_context(nc.semaphore(n))
        xg = sb("xg", [P, NS, d.D + d.E])
        xt_hi = sb("xt_hi", [P, d.KD, d.CAP], F32R)
        xt_lo = sb("xt_lo", [P, d.KD, d.CAP], F32R)
        gate = sb("gate", [P, NS])
        act_out = sb("act_out", [P, NS, BANK])
        hid = sb("hid", [P, NS, BANK])
        ht_hi = sb("ht_hi", [P, HF, d.CAP], F32R)
        ht_lo = sb("ht_lo", [P, HF, d.CAP], F32R)
        y = sb("y", [P, NS, d.D])
        one_hot = sb("one_hot", [P, d.NT, d.CAP], F16)
        slots = sb("slots", [P, d.CAP], F16)
        slots_i = sb("slots_i", [P, d.CAP], I32)
        token = sb("token", [P, d.NT], F16)
        token_i = sb("token_i", [P, d.NT], I32)
        index = [sb(f"index{s}", [P, 1], U32) for s in range(NS)]
        index_out = [sb(f"index_out{s}", [P, 1], U32) for s in range(NS)]
        row_g2 = sb("row_g2", [P, d.D])
        ps = {"A": psum("ps_a", [P, NS, BANK]), "B": psum("ps_b", [P, NS, BANK])}
        ps_t = [psum(f"ps_et{b}", [P, 2, d.CAP]) for b in range(TB)]
        ps_i = psum("ps_i", [P, BANK])

        row_loaded, counted, tables_done = sem("row_loaded"), sem("iotas"), sem("tables_done")
        hot, indexed, index_done = sem("hot"), sem("indexed"), sem("index_done")
        gathered, gate_done, scattered = sem("gathered"), sem("gate_done"), sem("scattered")
        index_kept = sem("index_kept")
        turned, hi_done, lo_done = sem("e_turned"), sem("e_hi_done"), sem("e_lo_done")
        activated, hid_done, y_done = sem("activated"), sem("hid_done"), sem("y_done")
        block = ctx.enter_context(nc.Block())

        ACTIVATE = {4 * c + 2: c for c in range(FC)}
        MULTIPLY = {4 * c + 4: c for c in range(FC)}
        TURN = {4 * c + 6: c for c in range(FC - 1)} | {4 * FC + 1: FC - 1}
        TURN_X = {4 * FC + 3: range(2 * FC, 2 * FC + 2), 4 * FC + 5: range(2 * FC + 2, FILLS)}
        INDEX, Y0 = 4, 4 * FC + 4

        def run(eng, body):
            body(0, True)
            with eng.Fori(1, LAST) as e:
                body(e, True)
            body(LAST, False)

        def fills_hid(c):
            return range(2 * c, 2 * c + 2)

        FILLS_X = range(2 * FC, FILLS)

        def split_fill(eng, e, f, kind):
            n = FILLS * e + f + d.KD // 2
            bank = ps_t[(f + d.KD // 2) % TB]
            hi, lo, at = (ht_hi, ht_lo, 2 * f) if f < 2 * FC else (xt_hi, xt_lo, 2 * (f - 2 * FC))
            if kind == "hi":
                eng.wait_ge(turned, n + 1)
                eng.activation(hi[:, at:at + 2, :], bank[:], ACT.Copy).then_inc(hi_done, 1)
            else:
                eng.wait_ge(hi_done, n + 1)
                eng.tensor_tensor(lo[:, at:at + 2, :], bank[:], hi[:, at:at + 2, :].bitcast(F32),
                                  ALU.subtract).then_inc(lo_done, 1)

        @block.sync
        def _(sp):
            sp.dma_start(row_g2[:], scratch["mod"][0:1, 5 * d.D:6 * d.D].broadcast_to([P, d.D])).then_inc(row_loaded, 16)

            def body(e, _):
                for n in range(stream.PIECES):
                    if not (isinstance(e, int) and e == 0 and n < stream.RAW):
                        stream.load(sp, e, n)
            run(sp, body)

        @block.gpsimd
        def _(pool):
            pool.iota(slots_i[:], [[1, d.CAP]], base=0, channel_multiplier=0).then_inc(counted, 1)
            pool.iota(token_i[:], [[P, d.NT]], base=0, channel_multiplier=1).then_inc(counted, 1)

            def gather(e):
                pool.wait_ge(index_done, e + 1)
                wait(pool, turned, FILLS * (e - 1) + d.KD // 2)
                wait(pool, gate_done, e)
                apart(pool, const["carried"])
                for s in range(NS):
                    pool.indirect_dma_start(xg[:, s, :], None, scratch["tok"],
                                            bass.IndirectOffsetOnAxis(ap=index[s][:], axis=0)).then_inc(gathered, 16)

            def body(e, more):
                wait(pool, scattered, 16 * NS * e)
                pool.wait_ge(index_done, e + 1)
                apart(pool, const["carried"])
                for s in range(NS):
                    last = pool.tensor_copy(index_out[s][:], index[s][:])
                last.then_inc(index_kept, 1)
                if more:
                    gather(e + 1)
                pool.wait_ge(index_kept, e + 1)
                pool.wait_ge(y_done, 2 * NS * (e + 1))
                apart(pool, const["carried"])
                for s in range(NS):
                    pool.indirect_dma_start(scratch["res"], bass.IndirectOffsetOnAxis(ap=index_out[s][:], axis=0),
                                            y[:, s, :], None, compute_op=ALU.add).then_inc(scattered, 16)
            gather(0)
            run(pool, body)
            pool.wait_ge(scattered, 16 * NS * d.E)

        @block.scalar
        def _(act):
            for f in FILLS_X:
                split_fill(act, -1, f, "hi")

            def body(e, more):
                for u in range(SUBS):
                    if u in ACTIVATE:
                        act.wait_ge(used, SUBS * e + u)
                        wait(act, hid_done, FC * e + ACTIVATE[u])
                        act.activation(act_out[:], ps["A"][:], ACT.Silu).then_inc(activated, 1)
                    if u in TURN:
                        for f in fills_hid(TURN[u]):
                            split_fill(act, e, f, "hi")
                    if u in TURN_X and more:
                        for f in TURN_X[u]:
                            split_fill(act, e, f, "hi")
                    if more or u + RING < SUBS:
                        convert(act, e, u + RING, "hi")
            run(act, body)

        @block.vector
        def _(dve):
            def make_hot(e):
                wait(dve, indexed, e)
                dve.tensor_tensor(one_hot[:], copies(slots[:], 1, d.NT),
                                  slot_of[:, :, bass.ds(e, 1)].broadcast_to([P, d.NT, d.CAP]),
                                  ALU.is_equal).then_inc(hot, 1)

            def take_index(e):
                dve.wait_ge(indexed, e + 1)
                wait(dve, gathered, 16 * NS * e)
                wait(dve, index_kept, e)
                for s in range(NS):
                    last = dve.tensor_copy(index[s][:], ps_i[:, s:s + 1])
                last.then_inc(index_done, 1)

            def weigh(e, c):
                dve.wait_ge(used, SUBS * e + Y0 + 4 * c)
                wait(dve, scattered, 16 * NS * e)
                for s in range(NS):
                    cols = slice(c * BANK, (c + 1) * BANK)
                    dve.scalar_tensor_tensor(out=y[:, s, cols], in0=ps["AB"[c]][:, s, :], scalar=gate[:, s:s + 1],
                                             in1=row_g2[:, cols], op0=ALU.mult, op1=ALU.mult).then_inc(y_done, 1)

            dve.wait_ge(counted, 2)
            dve.tensor_copy(slots[:], slots_i[:]).then_inc(tables_done, 1)
            dve.tensor_copy(token[:], token_i[:]).then_inc(tables_done, 1)
            dve.wait_ge(tables_done, 2)
            dve.wait_ge(row_loaded, 16)
            make_hot(0)
            take_index(0)
            for f in FILLS_X:
                split_fill(dve, -1, f, "lo")

            def body(e, more):
                for u in range(SUBS):
                    if u == 0:
                        if not isinstance(e, int) or e > 0:
                            weigh(e - 1, 1)
                        dve.wait_ge(gathered, 16 * NS * (e + 1))
                        wait(dve, y_done, 2 * NS * e)
                        dve.tensor_copy(gate[:], xg[:, :, bass.ds(d.D + e, 1)].rearrange("p s n -> p (s n)")).then_inc(gate_done, 1)
                    if u == 1 and more:
                        make_hot(e + 1)
                    if u in MULTIPLY:
                        c = MULTIPLY[u]
                        dve.wait_ge(used, SUBS * e + u)
                        dve.wait_ge(activated, FC * e + c + 1)
                        wait(dve, turned, FILLS * e + 2 * c + d.KD // 2)
                        dve.tensor_tensor(hid[:], ps["B"][:], act_out[:], ALU.mult).then_inc(hid_done, 1)
                    if u == INDEX and more:
                        take_index(e + 1)
                    if u in TURN:
                        for f in fills_hid(TURN[u]):
                            split_fill(dve, e, f, "lo")
                    if u == Y0:
                        dve.wait_ge(gate_done, e + 1)
                        weigh(e, 0)
                    if u in TURN_X and more:
                        for f in TURN_X[u]:
                            split_fill(dve, e, f, "lo")
                    if more or u + RING < SUBS:
                        convert(dve, e, u + RING, "lo")
            run(dve, body)
            weigh(LAST, 1)

        @block.tensor
        def _(pe):
            def find(e):
                pe.wait_ge(hot, e + 1)
                wait(pe, index_done, e)
                for s in range(NS):
                    for t in range(d.NT):
                        last = pe.matmul(ps_i[:, s:s + 1], one_hot[:, t, s * P:(s + 1) * P], token[:, t:t + 1],
                                         start=(t == 0), stop=(t == d.NT - 1))
                last.then_inc(indexed, 1)

            def turn(e, f, source):
                n = FILLS * e + f + d.KD // 2
                bank = ps_t[(f + d.KD // 2) % TB]
                wait(pe, lo_done, n - TB + 1)
                for k in range(2):
                    for s in range(NS):
                        last = pe.transpose(bank[:, k, s * P:(s + 1) * P], source(s, k), const["ident"][:])
                return last.then_inc(turned, 1)

            def turn_x(e, fills):
                pe.wait_ge(gathered, 16 * NS * (e + 2))
                for f in fills:
                    turn(e, f, lambda s, k: xg[:, s, (2 * (f - 2 * FC) + k) * P:(2 * (f - 2 * FC) + k + 1) * P])

            def turn_hid(e, c):
                pe.wait_ge(hid_done, FC * e + c + 1)
                for f in fills_hid(c):
                    turn(e, f, lambda s, k: hid[:, s, (2 * (f % 2) + k) * P:(2 * (f % 2) + k + 1) * P])

            pe.wait_ge(tables_done, 2)
            find(0)
            turn_x(-1, FILLS_X)

            def body(e, more):
                for u in range(SUBS):
                    n = SUBS * e + u
                    b = u % RING
                    if u == INDEX and more:
                        find(e + 1)
                    if u in TURN:
                        turn_hid(e, TURN[u])
                    if u in TURN_X and more:
                        turn_x(e, TURN_X[u])
                    first = u % 2 == 0 if u < 4 * FC else u % 4 == 0
                    stop = u % 2 == 1 if u < 4 * FC else u % 4 == 3
                    if u < 4 * FC:
                        acc, hi, lo, k0 = ps["AB"[u // 2 % 2]], xt_hi, xt_lo, KH * (u % 2)
                        if u == 0:
                            pe.wait_ge(lo_done, FILLS * e + d.KD // 2)
                            wait(pe, y_done, 2 * NS * (e - 1) + NS)
                        elif u == 2:
                            wait(pe, y_done, 2 * NS * e)
                        elif first:
                            c = u // 4
                            pe.wait_ge(activated if u % 4 == 0 else hid_done, FC * e + c)
                    else:
                        c, k0 = (u - 4 * FC) // 4, KH * (u % 4)
                        acc, hi, lo = ps["AB"[c]], ht_hi, ht_lo
                        if first:
                            pe.wait_ge(hid_done if c else activated, FC * (e + 1))
                        pe.wait_ge(lo_done, FILLS * e + d.KD // 2 + min(2 * (u % 4) + 2, 2 * FC))
                    pe.wait_ge(w_hi_done, n + 1)
                    pe.wait_ge(w_lo_done, n + 1)
                    for k in range(KH):
                        for s in range(NS):
                            rows = slice(s * P, (s + 1) * P)
                            for i, (x, w) in enumerate(((hi, w_hi), (hi, w_lo), (lo, w_hi))):
                                last = pe.matmul(acc[:, s, :], x[:, k0 + k, rows], w[b][:, k, :],
                                                 start=(first and k == 0 and i == 0), stop=(stop and k == KH - 1 and i == 2))
                    last.then_inc(used, 1)
            run(pe, body)



def final_norm(nc, d, io, scratch, const, out):
    NG = 4
    TG = d.NT // NG
    with ExitStack() as ctx:
        sb = lambda n, s, t=F32: ctx.enter_context(nc.sbuf_tensor(n, s, t))
        sem = lambda n: ctx.enter_context(nc.semaphore(n))
        r = sb("r_in", [P, d.NT, d.D])
        row_g = sb("row_g", [P, d.D])
        row_b = sb("row_b", [P, d.D])
        stats = sb("stats6", [P, TG, 2, 6])
        mean_var = sb("mean_var6", [P, TG, 2])
        var_eps = sb("var_eps6", [P, TG])
        rstd = sb("rstd6", [P, TG])
        shift = sb("shift6", [P, d.NT])
        scale = sb("scale6", [P, d.NT])
        minus_half = sb("minus_half6", [P, TG])
        rows_loaded, half_made = sem("rows_loaded6"), sem("half_made6")
        loaded = [sem(f"r_loaded{q}") for q in range(NG)]
        stats_done, mv_done, var_done, rstd_done, shift_done = (sem("stats_done6"), sem("mv_done6"), sem("var_done6"),
                                                                sem("rstd_done6"), sem("shift_done6"))
        norm_done, gain_done, out_done, stored = sem("norm_done6"), sem("gain_done6"), sem("out_done6"), sem("stored6")
        block = ctx.enter_context(nc.Block())

        def tiles(eng, q, step):
            with eng.Fori(q * TG, (q + 1) * TG) as t:
                step(t)

        def tile_of(ap, t):
            return ap[:, bass.ds(t, 1), :].rearrange("p t n -> p (t n)")

        @block.sync
        def _(sp):
            def load(q):
                sp.dma_start(r[:, q * TG:(q + 1) * TG, :], scratch["res"][q * TG * P:(q + 1) * TG * P, :]
                             .rearrange("(t p) n -> p t n", p=P)).then_inc(loaded[q], 16)

            load(0)
            for row, src in ((row_g, io["ln2_g"]), (row_b, io["ln2_b"])):
                sp.dma_start(row[:], src.broadcast_to([P, d.D])).then_inc(rows_loaded, 16)
            for q in range(1, NG):
                load(q)

            def step(t):
                sp.wait_ge(out_done, t + 1)
                sp.dma_start(out[0, bass.ds(t * P, P), :], tile_of(r, t)).then_inc(stored, 16)
            for q in range(NG):
                tiles(sp, q, step)
            sp.wait_ge(stored, 16 * d.NT)

        @block.gpsimd
        def _(pool):
            pool.memset(minus_half[:], -0.5).then_inc(half_made, 1)
            pool.wait_ge(half_made, 1)
            pool.wait_ge(rows_loaded, 32)

            def step(t):
                pool.wait_ge(gain_done, t + 1)
                pool.tensor_tensor(tile_of(r, t), tile_of(r, t), row_b[:], ALU.add).then_inc(out_done, 1)

            for q in range(NG + 1):
                if q < NG:
                    pool.wait_ge(var_done, q + 1)
                    wait(pool, shift_done, q)
                    pool.tensor_tensor(rstd[:], var_eps[:], minus_half[:], ALU.pow).then_inc(rstd_done, 1)
                if q > 0:
                    tiles(pool, q - 1, step)

        @block.scalar
        def _(act):
            def step(t):
                act.activation(tile_of(r, t), tile_of(r, t), ACT.Identity, scale=scale[:, bass.ds(t, 1)],
                               bias=shift[:, bass.ds(t, 1)]).then_inc(norm_done, 1)

            for q in range(NG):
                act.wait_ge(shift_done, q + 1)
                tiles(act, q, step)

        @block.vector
        def _(dve):
            def step(t):
                dve.wait_ge(norm_done, t + 1)
                dve.tensor_tensor(tile_of(r, t), tile_of(r, t), row_g[:], ALU.mult).then_inc(gain_done, 1)

            for q in range(NG + 1):
                if q < NG:
                    dve.wait_ge(loaded[q], 16)
                    for n in range(TG):
                        for half in range(2):
                            last = dve.bn_stats(stats[:, n, half, :], r[:, q * TG + n, half * BANK:(half + 1) * BANK])
                        last.then_inc(stats_done, 1)
                    for n in range(TG):
                        dve.wait_ge(stats_done, q * TG + n + 1)
                        dve.bn_aggr(mean_var[:, n, :], stats[:, n, :, :].rearrange("p a b -> p (a b)")).then_inc(mv_done, 1)
                    dve.wait_ge(mv_done, TG * (q + 1))
                    dve.tensor_scalar(var_eps[:], mean_var[:, :, 1], d.eps, None, ALU.add).then_inc(var_done, 1)
                if q == 1:
                    dve.wait_ge(rows_loaded, 32)
                if q > 0:
                    tiles(dve, q - 1, step)
                if q < NG:
                    group = slice(q * TG, (q + 1) * TG)
                    dve.wait_ge(rstd_done, q + 1)
                    dve.tensor_copy(scale[:, group], rstd[:])
                    dve.scalar_tensor_tensor(out=shift[:, group], in0=mean_var[:, :, 0], scalar=-1.0, in1=rstd[:],
                                             op0=ALU.mult, op1=ALU.mult).then_inc(shift_done, 1)


def trunk(nc, io, out):
    d = Dims(*[io[k] for k in ("x", "ctx", "ada_w", "attn_w_qkv", "attn_sink", "moe_router", "moe_w1")])
    scratch = {
        "mod": nc.dram_tensor("mod_scr", (2, d.MOD), F32).ap(),
        "qt": nc.dram_tensor("qt_scr", (d.NT, P, d.H, P), F32).ap(),
        "kt": nc.dram_tensor("kt_scr", (P, d.G, 2, (d.NT + 2) * P), F32).ap(),
        "tok": nc.dram_tensor("tok_scr", (d.T, d.D + d.E), F32).ap(),
        "res": nc.dram_tensor("res_scr", (d.T, d.D), F32).ap(),
        "v": nc.dram_tensor("v_scr", (d.NT + 2, P, d.G, 2 * d.DH), F32).ap(),
    }
    with ExitStack() as ctx:
        sb = lambda n, s, t=F32: ctx.enter_context(nc.sbuf_tensor(n, s, t))
        const = {"ident": sb("ident", [P, P]), "ident_bf": sb("ident_bf", [P, P], BF16),
                 "ones": sb("ones_col", [P, 1]), "c_act": sb("c_act", [P, 2, d.KD]),
                 "carried": ctx.enter_context(nc.semaphore("carried"))}
        k_ctx = sb("k_ctx", [P, d.G, 2, d.CTX], F32R)
        v_ctx = sb("v_ctx", [P, d.NC, d.G, 2 * d.DH], F32R)
        aff = sb("aff", [P, d.NT, d.E])
        made = ctx.enter_context(nc.semaphore("made"))
        with nc.Block() as block:
            @block.gpsimd
            def _(pool):
                pool.memset(const["ident"][:], 0.0).then_inc(made, 1)
                pool.memset(const["ident_bf"][:], 0.0).then_inc(made, 1)
                pool.memset(const["ones"][:], 1.0)
                pool.wait_ge(made, 2)
                for m in (const["ident"], const["ident_bf"]):
                    pool.affine_select(out=m[:], in_=m[:], compare_op=ALU.not_equal, fill=1.0, base=0,
                                       pattern=[[-1, P]], channel_multiplier=1)
        with ExitStack() as weights:
            wqkv_hi = weights.enter_context(nc.sbuf_tensor("wqkv_hi", [P, d.KD, d.QKV], F32R))
            wqkv_lo = weights.enter_context(nc.sbuf_tensor("wqkv_lo", [P, d.KD, d.QKV], F32R))
            for table in ("cos", "sin"):
                const[table] = weights.enter_context(nc.sbuf_tensor(table, [P, d.NT, d.DH], F32))
            modulation(nc, d, io, scratch, const, wqkv_hi, wqkv_lo)
            projection(nc, d, io, scratch, const, wqkv_hi, wqkv_lo, k_ctx, v_ctx)
        attention(nc, d, io, scratch, const, k_ctx, v_ctx, aff)
        slot_of = sb("slot_of", [P, d.NT, d.E])
        with ExitStack() as moe:
            stream = ExpertWeights(nc, d, io, moe)
            choice(nc, d, const, stream, aff, slot_of)
            experts(nc, d, io, scratch, const, stream, slot_of)
        final_norm(nc, d, io, scratch, const, out)



_INS = ["x", "c", "ctx", "c_ctx", "ada_w", "ada_b", "ln1_g", "ln1_b", "ln2_g", "ln2_b",
        "attn_w_qkv", "attn_sink", "attn_w_o", "moe_router", "moe_w1", "moe_w3", "moe_w2"]


def rotary_tables(tokens, head_dim, grid_w=64, base=10000.0):
    import numpy as np

    pos = np.arange(tokens)
    inv = (np.float32(base) ** (-np.arange(head_dim // 4, dtype=np.float32) / np.float32(head_dim // 4))).astype(np.float32)
    ang = np.concatenate([(pos // grid_w).astype(np.float32)[:, None] * inv,
                          (pos % grid_w).astype(np.float32)[:, None] * inv], axis=1)
    cos, sin = np.cos(ang), np.sin(ang)
    return np.concatenate([cos, cos], 1), np.concatenate([-sin, sin], 1)


def kernel(**inputs):
    import numpy as np
    import concourse.bacc as bacc
    from concourse.bass_utils import run_bass_kernel_spmd

    arrays = {name: np.ascontiguousarray(inputs[name]) for name in _INS}
    shape = arrays["x"].shape
    head_dim = shape[2] // arrays["attn_sink"].shape[1]
    arrays["cos"], arrays["sin"] = rotary_tables(shape[1], head_dim)
    nc = bacc.Bacc("TRN2", target_bir_lowering=False, num_devices=1)
    io = {name: nc.dram_tensor(f"in_{name}", a.shape, mybir.dt.from_np(a.dtype), kind="ExternalInput").ap()
          for name, a in arrays.items()}
    out = nc.dram_tensor("out_x", shape, F32, kind="ExternalOutput").ap()
    trunk(nc, io, out)
    r = run_bass_kernel_spmd(nc, [{f"in_{name}": a for name, a in arrays.items()}], core_ids=[0])
    return r.results[0]["out_x"]
```
